# Optimizing a Trainium2 kernel written in Bass

```python
import jax, jax.numpy as jnp
from jax import lax
import numpy as np

D_MODEL = 1024
BATCH = 1
SEQ = 512
DEPTH = 2

GRID_W = 64
CTX_LEN = 256
HEAD_DIM = 64
NORM_EPS = 1e-6
ROPE_BASE = 10000.0

POOL_WIDTH = 512
POOL_GROUPS = 4
POOL_WINDOWS = (2, 4, 8, 16)
POOL_GROUP_W = POOL_WIDTH // POOL_GROUPS

NA_HEADS = 8
NA_KH = 8
NA_KW = 16
NA_QC = 16
NA_KC = 32

SWA_HEADS = 8
SWA_KV_HEADS = 2
SWA_WINDOW = 128
SWA_BLOCK = 128

PEER_HEADS = 8
PEER_NKEYS = 128
PEER_EXPERTS = PEER_NKEYS * PEER_NKEYS
PEER_DKEY = 256
PEER_TOPK = 16
PEER_CHUNK = 128

NA_WIDTH = NA_HEADS * HEAD_DIM
SWA_Q_WIDTH = SWA_HEADS * HEAD_DIM
SWA_KV_WIDTH = SWA_KV_HEADS * HEAD_DIM
OFF_KN = 0
OFF_VN = OFF_KN + NA_WIDTH
OFF_KW = OFF_VN + NA_WIDTH
OFF_VW = OFF_KW + SWA_KV_WIDTH
CTX_KV_COLS = OFF_VW + SWA_KV_WIDTH
OFF_QN = CTX_KV_COLS
OFF_QW = OFF_QN + NA_WIDTH
OFF_A = OFF_QW + SWA_Q_WIDTH
OFF_G = OFF_A + POOL_WIDTH
IN_COLS = OFF_G + 3 * D_MODEL

kernel_name = 'hybrid_pool_natten_swa_peer_dit'

def rms_norm(x, g):
    xf = x.astype(jnp.float32)
    y = xf * lax.rsqrt(jnp.mean(xf * xf, axis=-1, keepdims=True) + NORM_EPS)
    return (y * g.astype(jnp.float32)).astype(x.dtype)

def modulate(h, shift, scale):
    return h * (1 + scale) + shift

def heads(z, off, n):
    return z[..., off:off + n * HEAD_DIM].reshape(*z.shape[:-1], n, HEAD_DIM)

def rope_axis(x, pos):
    f = x.shape[-1] // 2
    inv = ROPE_BASE ** (-jnp.arange(f, dtype=jnp.float32) / f)
    ang = pos.astype(jnp.float32)[:, None] * inv[None, :]
    cos = jnp.cos(ang)[None, :, None, :]
    sin = jnp.sin(ang)[None, :, None, :]
    xf = x.astype(jnp.float32)
    x1, x2 = xf[..., :f], xf[..., f:]
    return jnp.concatenate([x1 * cos - x2 * sin, x1 * sin + x2 * cos], axis=-1).astype(x.dtype)

def rope_2d(x, row, col):
    half = x.shape[-1] // 2
    return jnp.concatenate([rope_axis(x[..., :half], row), rope_axis(x[..., half:], col)], axis=-1)

def centred_pool_minus_self(a, w):
    T = a.shape[1]
    af = a.astype(jnp.float32)
    csum = jnp.concatenate([jnp.zeros_like(af[:, :1]), jnp.cumsum(af, axis=1)], axis=1)
    t = jnp.arange(T)
    lo = jnp.clip(t - w // 2, 0, T)
    hi = jnp.clip(t - w // 2 + w, 0, T)
    mean = (csum[:, hi] - csum[:, lo]) / (hi - lo).astype(jnp.float32)[None, :, None]
    return (mean - af).astype(a.dtype)

def pool_mixer(a, w_pool, pool_scale):
    B, T, _ = a.shape
    ag = a.reshape(B, T, POOL_GROUPS, POOL_GROUP_W)
    pooled = jnp.stack([centred_pool_minus_self(ag[:, :, g], w) for g, w in enumerate(POOL_WINDOWS)], axis=2)
    y = jnp.einsum('btgc,gce->btge', pooled, w_pool).reshape(B, T, POOL_WIDTH)
    return y * pool_scale

def neighbourhood_attention(q, k, v, k_ctx, v_ctx, rpb):
    B, S, H, d = q.shape
    rows = S // GRID_W
    kh = min(NA_KH, rows)
    ncb = GRID_W // NA_QC
    r = jnp.arange(rows)
    row_idx = jnp.clip(r - kh // 2, 0, rows - kh)[:, None] + jnp.arange(kh)[None, :]
    cb = jnp.arange(ncb)
    kcol_idx = jnp.clip(cb * NA_QC - NA_KW // 2, 0, GRID_W - NA_KC)[:, None] + jnp.arange(NA_KC)[None, :]
    qcol = cb[:, None] * NA_QC + jnp.arange(NA_QC)[None, :]
    qcol_start = jnp.clip(qcol - NA_KW // 2, 0, GRID_W - NA_KW)
    col_ok = (kcol_idx[:, None, :] >= qcol_start[:, :, None]) & (kcol_idx[:, None, :] < qcol_start[:, :, None] + NA_KW)
    dr = row_idx - r[:, None] + NA_KH - 1
    dc = jnp.clip(kcol_idx[:, None, :] - qcol[:, :, None] + NA_KW - 1, 0, 2 * NA_KW - 2)
    bias = rpb.astype(jnp.float32)[:, dr[:, None, None, :, None], dc[None, :, :, None, :]]
    scale = d ** -0.5
    qg = q.reshape(B, rows, ncb, NA_QC, H, d)
    kgrid = k.reshape(B, rows, GRID_W, H, d)
    vgrid = v.reshape(B, rows, GRID_W, H, d)
    kg = kgrid[:, row_idx[:, :, None, None], kcol_idx[None, None, :, :]]
    vg = vgrid[:, row_idx[:, :, None, None], kcol_idx[None, None, :, :]]
    s_loc = jnp.einsum('brnqhd,brinjhd->bhrnqij', qg, kg).astype(jnp.float32) * scale + bias[None]
    s_loc = jnp.where(col_ok[:, :, None, :], s_loc, -jnp.inf)
    s_loc = s_loc.reshape(B, H, rows, ncb, NA_QC, kh * NA_KC)
    s_ctx = jnp.einsum('brnqhd,bmhd->bhrnqm', qg, k_ctx).astype(jnp.float32) * scale
    p = jax.nn.softmax(jnp.concatenate([s_loc, s_ctx], axis=-1), axis=-1).astype(v.dtype)
    p_loc = p[..., :kh * NA_KC].reshape(B, H, rows, ncb, NA_QC, kh, NA_KC)
    p_ctx = p[..., kh * NA_KC:]
    o = jnp.einsum('bhrnqij,brinjhd->brnqhd', p_loc, vg) + jnp.einsum('bhrnqm,bmhd->brnqhd', p_ctx, v_ctx)
    return o.reshape(B, S, H * d)

def window_attention(q, k, v, k_ctx, v_ctx, sink):
    B, S, Hq, d = q.shape
    G = k.shape[2]
    rep = Hq // G
    L = k_ctx.shape[1]
    nb = S // SWA_BLOCK
    span = 3 * SWA_BLOCK
    scale = d ** -0.5
    qb = q.reshape(B, nb, SWA_BLOCK, G, rep, d)
    pad = ((0, 0), (SWA_BLOCK, SWA_BLOCK), (0, 0), (0, 0))
    kp = jnp.pad(k, pad)
    vp = jnp.pad(v, pad)
    idx = jnp.arange(nb)[:, None] * SWA_BLOCK + jnp.arange(span)[None, :]
    kwin = kp[:, idx]
    vwin = vp[:, idx]
    kpos = idx - SWA_BLOCK
    qpos = jnp.arange(nb)[:, None] * SWA_BLOCK + jnp.arange(SWA_BLOCK)[None, :]
    ok = (kpos[:, None, :] >= 0) & (kpos[:, None, :] < S) & (jnp.abs(qpos[:, :, None] - kpos[:, None, :]) <= SWA_WINDOW)
    s_loc = jnp.einsum('bnqgrd,bnkgd->bgrnqk', qb, kwin).astype(jnp.float32) * scale
    s_loc = jnp.where(ok, s_loc, -jnp.inf)
    s_ctx = jnp.einsum('bnqgrd,bmgd->bgrnqm', qb, k_ctx).astype(jnp.float32) * scale
    s_sink = jnp.broadcast_to(sink.astype(jnp.float32).reshape(G, rep)[None, :, :, None, None, None], s_loc.shape[:-1] + (1,))
    p = jax.nn.softmax(jnp.concatenate([s_loc, s_ctx, s_sink], axis=-1), axis=-1).astype(v.dtype)
    p_loc = p[..., :span]
    p_ctx = p[..., span:span + L]
    o = jnp.einsum('bgrnqk,bnkgd->bnqgrd', p_loc, vwin) + jnp.einsum('bgrnqm,bmgd->bnqgrd', p_ctx, v_ctx)
    return o.reshape(B, S, Hq * d)

def context_attention(q, k, v, sink=None):
    B, L, Hq, d = q.shape
    G = k.shape[2]
    rep = Hq // G
    qg = q.reshape(B, L, G, rep, d)
    s = jnp.einsum('blgrd,bmgd->bgrlm', qg, k).astype(jnp.float32) * (d ** -0.5)
    if sink is not None:
        s_sink = jnp.broadcast_to(sink.astype(jnp.float32).reshape(G, rep)[None, :, :, None, None], s.shape[:-1] + (1,))
        s = jnp.concatenate([s, s_sink], axis=-1)
    p = jax.nn.softmax(s, axis=-1)[..., :L].astype(v.dtype)
    o = jnp.einsum('bgrlm,bmgd->blgrd', p, v)
    return o.reshape(B, L, Hq * d)

def merge_branches(z, ya, yb, yc, w_out):
    g = jax.nn.sigmoid(z[..., OFF_G:OFF_G + 3 * D_MODEL]).reshape(*z.shape[:-1], 3, D_MODEL)
    m = g[..., 0, :] * ya + g[..., 1, :] * yb + g[..., 2, :] * yc
    return m @ w_out

def peer_ffn(h, w_q, sub_keys, u_tab, v_tab):
    lead = h.shape[:-1]
    hf = h.reshape(-1, D_MODEL)
    T = hf.shape[0]
    q = (hf @ w_q).reshape(T, PEER_HEADS, 2, PEER_DKEY // 2)
    s = jnp.einsum('thpc,hpkc->thpk', q, sub_keys).astype(jnp.float32)
    top_s, top_i = lax.top_k(s, PEER_TOPK)
    cand_s = top_s[:, :, 0, :, None] + top_s[:, :, 1, None, :]
    cand_i = top_i[:, :, 0, :, None] * PEER_NKEYS + top_i[:, :, 1, None, :]
    best_s, best_j = lax.top_k(cand_s.reshape(T, PEER_HEADS, PEER_TOPK * PEER_TOPK), PEER_TOPK)
    expert = jnp.take_along_axis(cand_i.reshape(T, PEER_HEADS, PEER_TOPK * PEER_TOPK), best_j, axis=-1)
    gate = jax.nn.softmax(best_s, axis=-1).astype(h.dtype)
    hk = PEER_HEADS * PEER_TOPK
    nc = T // PEER_CHUNK

    def chunk(args):
        xc, ec, gc = args
        u = u_tab[ec]
        vv = v_tab[ec]
        a = jnp.einsum('ced,cd->ce', u, xc)
        return jnp.einsum('ce,ced->cd', gc * jax.nn.gelu(a, approximate=False), vv)

    out = lax.map(chunk, (hf.reshape(nc, PEER_CHUNK, D_MODEL),
                          expert.reshape(nc, PEER_CHUNK, hk),
                          gate.reshape(nc, PEER_CHUNK, hk)))
    return out.reshape(*lead, D_MODEL)

def setup_inputs(seed: int = 0) -> dict:
    key = jax.random.key(seed)
    ks = jax.random.split(key, 24)
    f32 = jnp.float32
    nrm = lambda k, shape, s: jax.random.normal(k, shape, f32) * s
    return {
        'x': nrm(ks[0], (BATCH, SEQ, D_MODEL), 1.0),
        'c': nrm(ks[1], (BATCH, D_MODEL), 1.0),
        'ctx': nrm(ks[2], (BATCH, CTX_LEN, D_MODEL), 1.0),
        'c_ctx': nrm(ks[3], (D_MODEL,), 1.0),
        'ada_w': nrm(ks[4], (DEPTH, D_MODEL, 6 * D_MODEL), D_MODEL ** -0.5),
        'ada_b': nrm(ks[5], (DEPTH, 6 * D_MODEL), 0.02),
        'norm1_g': 1.0 + nrm(ks[6], (DEPTH, D_MODEL), 0.02),
        'norm2_g': 1.0 + nrm(ks[7], (DEPTH, D_MODEL), 0.02),
        'w_in': nrm(ks[8], (DEPTH, D_MODEL, IN_COLS), D_MODEL ** -0.5),
        'pool_w': nrm(ks[9], (DEPTH, POOL_GROUPS, POOL_GROUP_W, POOL_GROUP_W), POOL_GROUP_W ** -0.5),
        'pool_scale': 1.0 + nrm(ks[10], (DEPTH, POOL_WIDTH), 0.1),
        'na_rpb': nrm(ks[11], (DEPTH, NA_HEADS, 2 * NA_KH - 1, 2 * NA_KW - 1), 0.1),
        'swa_sink': nrm(ks[12], (DEPTH, SWA_HEADS), 0.5),
        'w_branch_a': nrm(ks[13], (DEPTH, POOL_WIDTH, D_MODEL), POOL_WIDTH ** -0.5),
        'w_branch_b': nrm(ks[14], (DEPTH, NA_WIDTH, D_MODEL), NA_WIDTH ** -0.5),
        'w_branch_c': nrm(ks[15], (DEPTH, SWA_Q_WIDTH, D_MODEL), SWA_Q_WIDTH ** -0.5),
        'w_out': nrm(ks[16], (DEPTH, D_MODEL, D_MODEL), D_MODEL ** -0.5),
        'peer_wq': nrm(ks[17], (DEPTH, D_MODEL, PEER_HEADS * PEER_DKEY), D_MODEL ** -0.5),
        'peer_keys': nrm(ks[18], (DEPTH, PEER_HEADS, 2, PEER_NKEYS, PEER_DKEY // 2), (PEER_DKEY // 2) ** -0.5),
        'peer_u': nrm(ks[19], (DEPTH, PEER_EXPERTS, D_MODEL), D_MODEL ** -0.5),
        'peer_v': nrm(ks[20], (DEPTH, PEER_EXPERTS, D_MODEL), 0.5),
        'final_g': 1.0 + nrm(ks[21], (D_MODEL,), 0.02),
    }

def reference(x, c, ctx, c_ctx, ada_w, ada_b, norm1_g, norm2_g, w_in, pool_w, pool_scale,
              na_rpb, swa_sink, w_branch_a, w_branch_b, w_branch_c, w_out,
              peer_wq, peer_keys, peer_u, peer_v, final_g):
    S = x.shape[1]
    t = jnp.arange(S)
    row = t // GRID_W
    col = t % GRID_W
    xc = ctx
    for l in range(DEPTH):
        last = l == DEPTH - 1
        mod_l = jax.nn.silu(c) @ ada_w[l] + ada_b[l]
        mod_c = jax.nn.silu(c_ctx) @ ada_w[l] + ada_b[l]
        sh1, sc1, gt1, sh2, sc2, gt2 = jnp.split(mod_l[:, None, :], 6, axis=-1)
        csh1, csc1, cgt1, csh2, csc2, cgt2 = jnp.split(mod_c, 6, axis=-1)

        h = modulate(rms_norm(x, norm1_g[l]), sh1, sc1)
        hc = modulate(rms_norm(xc, norm1_g[l]), csh1, csc1)
        z = h @ w_in[l]
        zc = hc @ (w_in[l][:, :CTX_KV_COLS] if last else w_in[l])
        kn_c = heads(zc, OFF_KN, NA_HEADS)
        vn_c = heads(zc, OFF_VN, NA_HEADS)
        kw_c = heads(zc, OFF_KW, SWA_KV_HEADS)
        vw_c = heads(zc, OFF_VW, SWA_KV_HEADS)

        qn = heads(z, OFF_QN, NA_HEADS)
        kn = heads(z, OFF_KN, NA_HEADS)
        vn = heads(z, OFF_VN, NA_HEADS)
        qw = rope_2d(heads(z, OFF_QW, SWA_HEADS), row, col)
        kw = rope_2d(heads(z, OFF_KW, SWA_KV_HEADS), row, col)
        vw = heads(z, OFF_VW, SWA_KV_HEADS)
        ya = pool_mixer(z[..., OFF_A:OFF_G], pool_w[l], pool_scale[l]) @ w_branch_a[l]
        yb = neighbourhood_attention(qn, kn, vn, kn_c, vn_c, na_rpb[l]) @ w_branch_b[l]
        yc = window_attention(qw, kw, vw, kw_c, vw_c, swa_sink[l]) @ w_branch_c[l]
        x = x + gt1 * merge_branches(z, ya, yb, yc, w_out[l])
        if not last:
            ya_c = pool_mixer(zc[..., OFF_A:OFF_G], pool_w[l], pool_scale[l]) @ w_branch_a[l]
            yb_c = context_attention(heads(zc, OFF_QN, NA_HEADS), kn_c, vn_c) @ w_branch_b[l]
            yc_c = context_attention(heads(zc, OFF_QW, SWA_HEADS), kw_c, vw_c, swa_sink[l]) @ w_branch_c[l]
            xc = xc + cgt1 * merge_branches(zc, ya_c, yb_c, yc_c, w_out[l])

        h2 = modulate(rms_norm(x, norm2_g[l]), sh2, sc2)
        x = x + gt2 * peer_ffn(h2, peer_wq[l], peer_keys[l], peer_u[l], peer_v[l])
        if not last:
            h2c = modulate(rms_norm(xc, norm2_g[l]), csh2, csc2)
            xc = xc + cgt2 * peer_ffn(h2c, peer_wq[l], peer_keys[l], peer_u[l], peer_v[l])
    return rms_norm(x, final_g)


_drawn_inputs = setup_inputs


def setup_inputs(seed=0):
    import zlib

    import numpy as np

    out = dict(_drawn_inputs(seed))
    spreads = {}
    factors = {'swa_sink': 8.0, 'final_g': 7.55, 'na_rpb': 2.688}
    for name, (base, spread) in spreads.items():
        noise = np.random.default_rng([zlib.crc32(name.encode()), seed]).standard_normal(out[name].shape)
        drawn = base * np.exp(spread * noise) if base else spread * noise
        out[name] = __import__('jax').numpy.asarray(drawn.astype(out[name].dtype))
    for name, factor in factors.items():
        out[name] = (out[name] * factor).astype(out[name].dtype)
    return out
```

```python
from contextlib import ExitStack, contextmanager

import concourse.bass as bass
from concourse import mybir

F32 = mybir.dt.float32
U32 = mybir.dt.uint32
ALU = mybir.AluOpType
ACT = mybir.ActivationFunctionType
AX = mybir.AxisListType

P = 128
D = 1024
KB = D // P
DEPTH = 2
SEQ, CTX = 512, 256
TOK = SEQ + CTX
LT, CT = SEQ // P, CTX // P
NT = LT + CT
GRID_W, QC, KC = 64, 16, 32
ROWS = SEQ // GRID_W
NCB = GRID_W // QC
HD = 64
PAIRS = 4
TW = 48
MODS = 6 * D
MCH = MODS // 512
POOLS = (2, 4, 8, 16)
PADL = 8
PADW = PADL + SEQ + PADL + PADL + CTX + PADL
HEADS, TOPK, NKEYS = 8, 16, 128
RING = 8
ITS = HEADS
SCALE = HD ** -0.5
EPS = 1e-6
LOW = -3.0e38
MASKED = -1.0e30
DB = KB // 2


def live_tiles(l):
    return NT if l < DEPTH - 1 else LT


def token_groups(l):
    return [(0, SEQ), (SEQ, CTX)] if l < DEPTH - 1 else [(0, SEQ)]


def key_start(n):
    return min(max(n * QC - 8, 0), GRID_W - KC)


class Steps:

    def __init__(self, eng, sem):
        self.eng, self.sem, self.n, self.at = eng, sem, 0, 0

    def done(self, instruction, held=None):
        instruction.then_inc(self.sem, 1)
        self.n += 1
        self.eng.wait_ge(self.sem, self.at + self.n)
        if held:
            self.eng.sem_inc(held, 1)

    @contextmanager
    def loop(self, count, per):
        first, outer = self.n, self.at
        with self.eng.Fori(0, count) as i:
            self.at = outer + i * per
            yield i
            assert self.n - first == per, f"the loop takes {self.n - first} steps"
        self.at = outer
        self.n = first + count * per


def build(nc, t):
    with ExitStack() as ctx:
        sb = lambda name, shape, dt=F32: ctx.enter_context(nc.sbuf_tensor(name, shape, dt))
        sem = lambda name: ctx.enter_context(nc.semaphore(name))
        per_layer = lambda name: [sem(f"{name}{l}") for l in range(DEPTH)]

        X = sb("X", [P, NT, D])
        H = sb("H", [P, NT, D])
        arena = sb("arena", [P, 33280])
        modb = sb("modb", [P, 4, D])
        gt = sb("gt", [P, 2, D])
        ident = sb("ident", [P, P])
        rope_cos = sb("rope_cos", [P, LT, HD])
        rope_sin = sb("rope_sin", [P, LT, HD])
        na_mask = sb("na_mask", [P, NCB, KC])
        swa_mask = sb("swa_mask", [P, 2, P])
        iota = sb("iota", [P, TOPK])
        sinks = sb("sinks", [P, 8])
        sink_st = sb("sink_st", [P, 2])
        ss = sb("ss", [P, 3, 8])
        att = sb("att", [P, 8, 4])
        csil = sb("csil", [P, KB, 2])
        PS = ctx.enter_context(nc.psum_tensor("PS", [P, 8, 512], F32))
        PSF = PS[:].rearrange("p b n -> p (b n)")

        def view(at, *dims):
            n = 1
            for d in dims:
                n *= d
            v = arena[:, at:at + n]
            if len(dims) == 2:
                return v.rearrange("p (a b) -> p a b", b=dims[1])
            if len(dims) == 3:
                return v.rearrange("p (a b c) -> p a b c", b=dims[1], c=dims[2])
            return v

        hT = view(27136, KB, TOK)
        qwT = view(0, PAIRS, TOK)
        kwT = view(3072, 2, TOK)
        Vw = view(4608, NT, P)
        VN = view(5376, 10, 512)
        oT = [view(10496 + 3072 * b, PAIRS, TOK) for b in range(3)]
        w_tok = view(10496, 10240)
        vn_st = view(20736, 2, 512)
        kdup = view(21760, 2, 2 * P)
        q_rot = view(22272, 2, 512)
        r_tmp = view(23296, 512)
        k_rot = view(23808, P)
        wqk = view(19712, 2, KB, P)
        k_st = view(21760, TOK)
        q_st = view(22528, TOK)
        prob = view(23296, 2, 640)
        probT = view(24576, 2, 5 * P)
        o_sb = view(25856, 2, P)
        rpbT = H[:].rearrange("p a b -> p (a b)")[:, 0:8 * ROWS * TW].rearrange(
            "p (h r w) -> p h r w", h=8, r=ROWS)
        a_pad = view(5376, PADW)
        win = view(6176, 2, PADW)
        inv_n = view(7776, TOK)
        pooled = view(8544, TOK)
        wa = view(19712, 2, KB, P)
        wpool = view(23296, PAIRS, P)
        pscale = view(23808, PAIRS)
        mT = view(0, KB, TOK)
        sig = view(6144, 2, TOK)
        mtmp = view(7680, TOK)
        wgb = [view(19712, 36, P), H[:].rearrange("p a b -> p (a b)")[:, 0:36 * P].rearrange("p (a b) -> p a b", b=P)]
        wout = view(10496, KB, D)
        xtmp = view(7680, 2, 512)
        sq_tmp = view(18688, D)
        S_all = view(0, 12544)
        wqs = view(12544, 2, 9, P)
        qb = view(14848, 2, TOK)
        U = view(12544, RING, D)
        V = view(12544 + RING * D, RING, D)
        at = 12544 + 2 * RING * D
        h_st = view(at, D)
        x_upd = view(at + 1024, D)
        diag = view(at + 2048, 4, P)
        s_st = view(at + 2560, 2, P)
        s_cut = view(at + 2816, 2, P)
        cand = view(at + 3072, 16, 16)
        cand_cut = view(at + 3328, 16, 16)
        onehot = view(at + 3584, 16, 32)
        assert at + 4256 <= 33280
        v16 = sb("v16", [P, 2, TOPK])
        i16 = sb("i16", [P, 2, TOPK], U32)
        code = sb("code", [P, 2 * TOPK])
        best = sb("best", [P, TOPK])
        best_j = sb("best_j", [P, TOPK], U32)
        ab_u = sb("ab_u", [P, TOPK, 2], U32)
        ab = sb("ab", [P, TOPK, 2])
        expert_f = sb("expert_f", [P, TOPK])
        expert_u = sb("expert_u", [P, 2, TOPK], U32)
        expert_v = sb("expert_v", [P, 2, TOPK], U32)
        top_ex = view(at + 4160, 2, TOPK)
        gate = view(at + 4192, 2, TOPK)
        act_in = view(at + 4224, 2, TOPK)
        act_out = view(at + 4096, 2, TOPK)
        wgt = view(at + 4128, 2, TOPK)
        red = sb("red", [P, 4])
        ada = [view(4096 * r, KB, 512) for r in range(2)]
        mrow = view(8192, 2, 3 * 512)
        mout = view(11264, 2, 512)

        s_const, s_x = sem("s_const"), sem("s_x")
        s_dve = sem("s_dve")
        s_ada = [sem(f"s_ada{r}") for r in range(2)]
        s_sg, s_silu = sem("s_sg"), sem("s_silu")
        s_mz, s_mod = sem("s_mz"), sem("s_mod")
        s_mst = [sem(f"s_mst{r}") for r in range(2)]
        norms = 2 * DEPTH + 1
        n_in = [sem(f"n_in{i}") for i in range(norms)]
        n_ss, n_sq = sem("n_ss"), sem("n_sq")
        n_h, n_t, n_c = sem("n_h"), sem("n_t"), sem("n_c")
        s_wt = [[sem(f"s_wt{l}{c}") for c in range(3)] for l in range(DEPTH)]
        s_tz = [sem(f"s_tz{c}") for c in range(3)]
        s_vst, s_kd, s_qd, s_bt, s_bc = [sem(x) for x in ("s_vst", "s_kd", "s_qd", "s_bt", "s_bc")]
        s_vout = [sem(f"s_vout{r}") for r in range(2)]
        s_vn, s_rpb, s_sink = per_layer("s_vn"), per_layer("s_rpb"), per_layer("s_sink")
        s_wqk = sem("s_wqk")
        a_z, a_zc, a_sk = sem("a_z"), sem("a_zc"), sem("a_sk")
        a_s, a_nm, a_p, a_t, a_pt, a_o, a_on, a_ot, a_oc = [
            sem(x) for x in ("a_s", "a_nm", "a_p", "a_t", "a_pt", "a_o", "a_on", "a_ot", "a_oc")]
        p_w, p_in, p_inv = [sem("p_w0"), sem("p_w1")], sem("p_in"), sem("p_inv")
        p_pad, p_z, p_c, p_pool, p_y, p_ya = [sem(x) for x in ("p_pad", "p_z", "p_c", "p_pool", "p_y", "p_ya")]
        m_w = [sem("m_w0"), sem("m_w1")]
        m_z, m_y, m_sig, m_m = sem("m_z"), sem("m_y"), sem("m_sig"), sem("m_m")
        s_wo, g_z, g_x = sem("s_wo"), sem("g_z"), sem("g_x")
        q_w = [sem("q_w0"), sem("q_w1")]
        q_z, q_c, q_s, q_sc = sem("q_z"), sem("q_c"), sem("q_s"), sem("q_sc")
        g_u = [sem(f"g_u{r}") for r in range(RING)]
        g_v = [sem(f"g_v{r}") for r in range(RING)]
        u_free, v_free = sem("u_free"), sem("v_free")
        f_idx, f_vidx, f_nm, f_ex, f_gel, f_w, f_dg, f_acc = [
            sem(x) for x in ("f_idx", "f_vidx", "f_nm", "f_ex", "f_gel", "f_w", "f_dg", "f_acc")]
        s_store = sem("s_store")
        s_held = sem("s_held")

        def before(l, per):
            return sum(per(m) for m in range(l))

        NORM_TILES = [n for l in range(DEPTH) for n in (NT, live_tiles(l))] + [LT]
        HT_TILES = NORM_TILES[:-1] + [0]
        n_base = [sum(NORM_TILES[:i]) for i in range(norms + 1)]
        c_base = [2 * sum(HT_TILES[:i]) for i in range(norms + 1)]
        ngr = lambda l: len(token_groups(l))
        bt_count = lambda l: NT + live_tiles(l)
        q_base = [before(l, live_tiles) for l in range(DEPTH + 1)]
        bt_base = [before(l, bt_count) for l in range(DEPTH + 1)]
        py_base = [before(l, lambda m: PAIRS * ngr(m)) for l in range(DEPTH + 1)]
        gx_base = [before(l, lambda m: 2 * live_tiles(m)) for l in range(DEPTH + 1)]
        qz_base = [before(l, lambda m: 2 * HEADS * ngr(m)) for l in range(DEPTH + 1)]
        it_base = [before(l, lambda m: HEADS * live_tiles(m)) for l in range(DEPTH + 1)]

        NA, SWA = 0, 1

        def units(l, kind):
            out = []
            for n in range(NCB):
                for hh in range(2):
                    if kind == NA:
                        out.append(("lat", hh, n, 512 - 2 * P))
                    else:
                        blocks = min(n + 2, LT) - max(n - 1, 0)
                        out.append(("lat", hh, n, 512 - blocks * P))
            if l < DEPTH - 1:
                for n in range(CT):
                    for hh in range(2):
                        out.append(("ctx", hh, n, 512))
            return out

        UN = [len(units(l, NA)) for l in range(DEPTH)]
        ZN = [4, 3]

        def unit_base(l, kind):
            return 2 + sum(2 * PAIRS * UN[m] for m in range(l)) + kind * PAIRS * UN[l]

        def pair_base(l, kind):
            return (2 * l + kind) * PAIRS

        def z_base(l):
            return 1 + sum(PAIRS * ZN[m] for m in range(l))

        def q_tokens(kind, what, n):
            if what == "ctx":
                return lambda ap: ap[:, SEQ + n * P:SEQ + (n + 1) * P]
            if kind == SWA:
                return lambda ap: ap[:, n * P:(n + 1) * P]
            return lambda ap: ap[:, 0:SEQ].rearrange("p (r c) -> p r c", c=GRID_W)[:, :, n * QC:(n + 1) * QC]

        @contextmanager
        def pair_loop(eng, kind, steps=None, per=0):
            if kind == NA:
                with (steps.loop(PAIRS, per) if steps else eng.Fori(0, PAIRS)) as p:
                    yield p, None
            else:
                with (steps.loop(2, 2 * per) if steps else eng.Fori(0, 2)) as g:
                    with (steps.loop(2, per) if steps else eng.Fori(0, 2)) as pp:
                        yield g * 2 + pp, g

        def rounds(eng, l, body, steps=None, per=0):
            n = HEADS * live_tiles(l)
            body(0, 0, True, False)
            with (steps.loop((n - 2) // 2, 2 * per) if steps else eng.Fori(0, (n - 2) // 2)) as i:
                body(i * 2 + 1, 1, False, False)
                body(i * 2 + 2, 0, False, False)
            body(n - 1, 1, False, True)

        block = ctx.enter_context(nc.Block())

        @block.sync
        def _(sp):
            for signal in (a_t, a_pt, a_o, a_on):
                sp.sem_inc(signal, 2)
            for signal in (a_s, a_nm, a_p):
                sp.sem_inc(signal, 2)
            for signal in (a_ot, a_oc, a_z, a_zc, s_mod, *s_mst):
                sp.sem_inc(signal, 1)
            for dst, name in ((ident, "ident"), (rope_cos, "rope_cos"), (rope_sin, "rope_sin"),
                              (na_mask, "na_mask"), (swa_mask, "swa_mask"), (iota, "iota"), (csil, "cc")):
                sp.dma_start(dst[:], t[name]).then_inc(s_const, 16)
            sp.dma_start(X[:, 0:LT, :], t["x"][0].rearrange("(t p) d -> p t d", p=P)).then_inc(s_x, 16)
            sp.dma_start(X[:, LT:NT, :], t["ctx"][0].rearrange("(t p) d -> p t d", p=P)).then_inc(s_x, 16)

            for r in range(2):
                sp.dma_start(ada[r], t["ada"][r]).then_inc(s_ada[r], 16)
                sp.dma_start(mrow[0:2, r, :], t["mrow"][r]).then_inc(s_ada[r], 16)
            with sp.Fori(0, DEPTH * MCH // 2 - 1) as i:
                for r in range(2):
                    sp.wait_ge(s_mod, 2 * i + (r + 2))
                    sp.dma_start(ada[r], t["ada"][2 * i + r + 2]).then_inc(s_ada[r], 16)
                    sp.dma_start(mrow[0:2, r, :], t["mrow"][2 * i + r + 2]).then_inc(s_ada[r], 16)

            def norm_rows(l, which):
                for v in range(2):
                    for dst, part in ((modb[:, 2 * v], 0), (modb[:, 2 * v + 1], 1), (gt[:, v], 2)):
                        for a in range(2):
                            row = t["mods_d"][l * MCH + 2 * (3 * which + part) + a, v:v + 1, :]
                            sp.dma_start(dst[:, a * 512:(a + 1) * 512], row.to_broadcast([P, 512])).then_inc(
                                n_in[2 * l + which], 16)

            for r in range(2):
                sp.wait_ge(s_mst[r], 1 + 16 * DEPTH * MCH // 2)
            for l in range(DEPTH):
                nt, ng = live_tiles(l), ngr(l)
                if l:
                    sp.wait_ge(f_acc, 2 + it_base[l])
                norm_rows(l, 0)
                sp.dma_start(sinks[:], t["sink"][l:l + 1, :].to_broadcast([P, 8])).then_inc(s_sink[l], 16)
                o = 0
                for c, n in enumerate((512, 256, 512)):
                    sp.dma_start(w_tok[:, o:o + KB * n], t["w_tok"][l, :, o:o + KB * n]).then_inc(s_wt[l][c], 16)
                    o += KB * n
                for i in range(NT):
                    sp.wait_ge(s_vst, l * NT + i + 1)
                    sp.dma_start(t["vn_d"][l, i * P:(i + 1) * P, :], vn_st[:, i % 2, :]).then_inc(s_vout[i % 2], 16)
                for r in range(2):
                    sp.wait_ge(s_vout[r], 16 * (l + 1) * NT // 2)
                grid = t["vn_d"][l, 0:SEQ, :].rearrange("(r c) d -> r c d", c=GRID_W)
                for n in range(NCB):
                    for half in range(2):
                        for r in range(4):
                            sp.dma_start(VN[r * KC:(r + 1) * KC, 2 * n + half, :],
                                         grid[4 * half + r, key_start(n):key_start(n) + KC, :]).then_inc(s_vn[l], 16)
                for i in range(CT):
                    sp.dma_start(VN[:, 8 + i, :], t["vn_d"][l, SEQ + i * P:SEQ + (i + 1) * P, :]).then_inc(s_vn[l], 16)
                sp.wait_ge(n_t, c_base[2 * l + 1])
                sp.dma_start(rpbT, t["rpb"][l]).then_inc(s_rpb[l], 16)
                sp.wait_ge(s_tz[0], (l + 1) * NT)
                sp.wait_ge(s_tz[1], (l + 1) * NT)
                sp.wait_ge(s_tz[2], q_base[l + 1])
                with sp.Fori(0, PAIRS) as p:
                    sp.wait_ge(a_z, z_base(l) + p * ZN[l])
                    sp.dma_start(wqk, t["wqk"][p + l * PAIRS]).then_inc(s_wqk, 16)
                sp.wait_ge(a_oc, (unit_base(l, SWA) + PAIRS * UN[l]) // 2)
                sp.dma_start(wpool, t["pool_w"][l]).then_inc(p_in, 16)
                sp.dma_start(pscale, t["pool_scale"][l]).then_inc(p_in, 16)
                for g in range(PAIRS):
                    if g >= 2:
                        sp.wait_ge(p_z, l * PAIRS + g - 1)
                    sp.dma_start(wa[:, g % 2], t["wa"][l, g]).then_inc(p_w[g % 2], 16)
                    if g:
                        sp.wait_ge(p_pool, l * PAIRS + g)
                    sp.dma_start(inv_n, t["inv_n"][g:g + 1, :].to_broadcast([P, TOK])).then_inc(p_inv, 16)
                sp.wait_ge(p_ya, py_base[l + 1])
                for r in range(2):
                    sp.dma_start(wgb[r], t["wgb"][l * KB + r]).then_inc(m_w[r], 16)
                with sp.Fori(0, KB // 2 - 1) as i:
                    for r in range(2):
                        sp.wait_ge(m_y, 3 * KB * l + 6 * i + 3 * r + 3)
                        sp.dma_start(wgb[r], t["wgb"][2 * i + (l * KB + r + 2)]).then_inc(m_w[r], 16)
                sp.wait_ge(m_y, 3 * KB * (l + 1))
                sp.dma_start(wout, t["w_out"][l]).then_inc(s_wo, 16)
                sp.wait_ge(g_x, gx_base[l + 1])
                norm_rows(l, 1)
                for r in range(2):
                    sp.dma_start(wqs[:, r], t["wqs"][l * 2 * HEADS + r]).then_inc(q_w[r], 16)
                with sp.Fori(0, HEADS - 1) as i:
                    for r in range(2):
                        sp.wait_ge(q_s, 2 * HEADS * l + 2 * i + (r + 1))
                        sp.dma_start(wqs[:, r], t["wqs"][2 * i + (l * 2 * HEADS + r + 2)]).then_inc(q_w[r], 16)
            sp.wait_ge(n_h, n_base[2 * DEPTH])
            sp.dma_start(modb[:, 0, :], t["final_g"].unsqueeze(0).to_broadcast([P, D])).then_inc(n_in[2 * DEPTH], 16)
            for k in range(LT):
                sp.wait_ge(n_h, n_base[2 * DEPTH] + k + 1)
                sp.dma_start(t["out"][0, k * P:(k + 1) * P, :], H[:, k, :]).then_inc(s_store, 16)
            sp.wait_ge(s_store, 16 * LT)

        @block.tensor
        def _(pe):
            pe.wait_ge(s_silu, 1)
            with pe.Fori(0, DEPTH * MCH // 2) as i:
                for r in range(2):
                    pe.wait_ge(s_ada[r], 32 * i + 32)
                    pe.wait_ge(s_mod, 2 * i + 1)
                    for k in range(KB):
                        mm = pe.matmul(PS[0:2, r, :], csil[:, k, :], ada[r][:, k, :], start=k == 0, stop=k == KB - 1)
                    mm.then_inc(s_mz, 1)

            def norm(i, tiles):
                for k in range(tiles):
                    pe.wait_ge(n_h, n_base[i] + k + 1)
                    for half in range(2):
                        x = 2 * k + half
                        if x >= 4:
                            pe.wait_ge(n_c, c_base[i] + x - 3)
                        for b in range(4):
                            mm = pe.transpose(PS[:, x % 4, b * P:(b + 1) * P],
                                              H[:, k, (4 * half + b) * P:(4 * half + b + 1) * P], ident[:])
                        mm.then_inc(n_t, 1)

            def tokens(l):
                nt = live_tiles(l)
                pe.wait_ge(n_c, c_base[2 * l + 1])

                def turn(k):
                    pe.wait_ge(s_kd, l * NT + k + 1)
                    if k:
                        pe.wait_ge(s_bc, bt_base[l] + k + min(k, nt))
                    for g in range(2):
                        mm = pe.transpose(PS[:, 6, g * P:(g + 1) * P], kdup[:, k % 2, g * P:(g + 1) * P], ident[:])
                    mm.then_inc(s_bt, 1)
                    if k < nt:
                        pe.wait_ge(s_qd, q_base[l] + k + 1)
                        for b in range(PAIRS):
                            mm = pe.transpose(PS[:, 7, b * P:(b + 1) * P], q_rot[:, k % 2, b * P:(b + 1) * P], ident[:])
                        mm.then_inc(s_bt, 1)

                for k in range(NT):
                    o = 0
                    for c, n in enumerate((512, 256, 512)):
                        w = w_tok[:, o:o + KB * n].rearrange("p (k n) -> p k n", n=n)
                        o += KB * n
                        if c == 2 and k >= nt:
                            continue
                        if k == 0:
                            pe.wait_ge(s_wt[l][c], 16)
                        if k >= 2:
                            if c == 0:
                                pe.wait_ge(s_vst, l * NT + k - 1)
                            elif c == 1:
                                pe.wait_ge(s_kd, l * NT + k - 1)
                            else:
                                pe.wait_ge(s_qd, q_base[l] + k - 1)
                        for kb in range(KB):
                            mm = pe.matmul(PS[:, 3 * (k % 2) + c, 0:n], hT[:, kb, k * P:(k + 1) * P], w[:, kb, :],
                                           start=kb == 0, stop=kb == KB - 1)
                        mm.then_inc(s_tz[c], 1)
                    if k:
                        turn(k - 1)
                turn(NT - 1)
                pe.wait_ge(s_vst, (l + 1) * NT)
                pe.wait_ge(s_bc, bt_base[l + 1])

            def attention(l, kind):
                U = UN[l]
                todo = units(l, kind)
                if kind == NA:
                    pe.wait_ge(s_vn[l], 16 * (8 * 4 + CT))
                with pair_loop(pe, kind) as (p, g):
                    if kind == NA:
                        pe.wait_ge(s_wqk, 16 * p + 16 * (l * PAIRS + 1))
                        for bank, (side, t0, n) in enumerate(((1, 0, SEQ), (1, SEQ, CTX), (0, 0, SEQ), (0, SEQ, CTX))[:ZN[l]]):
                            for k in range(KB):
                                mm = pe.matmul(PS[:, bank, 0:n], wqk[:, side, k, :], hT[:, k, t0:t0 + n],
                                               start=k == 0, stop=k == KB - 1)
                            mm.then_inc(a_z, 1)
                        pe.wait_ge(a_zc, z_base(l) + ZN[l] + p * ZN[l])
                    else:
                        pe.wait_ge(a_sk, 2 * (l * PAIRS + 1) + p * 2)
                    ub = unit_base(l, kind) + p * U
                    ob = unit_base(l, kind) // 2 + p * (U // 2)
                    for u in range(U + 3):
                        if u < U:
                            what, hh, n, s0 = todo[u]
                            ks, qs = k_st[hh * HD:(hh + 1) * HD], q_st[hh * HD:(hh + 1) * HD]
                            at = 1024 * (u % 2)
                            lhs = qs[:, (SEQ if what == "ctx" else 0) + n * P:(SEQ if what == "ctx" else 0) + (n + 1) * P]
                            if u >= 2:
                                pe.wait_ge(a_p, ub + (u - 1))
                            if what == "lat":
                                if kind == NA:
                                    rhs = ks[:, 0:SEQ].rearrange("p (r c) -> p r c", c=GRID_W)[
                                        :, :, key_start(n):key_start(n) + KC]
                                else:
                                    rhs = ks[:, max(n - 1, 0) * P:min(n + 2, LT) * P]
                                pe.matmul(PSF[:, at + s0:at + 512], lhs, rhs, start=True, stop=True)
                            pe.matmul(PSF[:, at + 512:at + 768], lhs, ks[:, SEQ:TOK], start=True, stop=True).then_inc(a_s, 1)
                        w = u - 1
                        if 0 <= w < U:
                            blocks = (768 - todo[w][3]) // P
                            pe.wait_ge(a_p, ub + (w + 1))
                            if w >= 1:
                                pe.wait_ge(a_pt, ub + w)
                            for b in range(5 - blocks, 5):
                                mm = pe.transpose(PSF[:, 2048 + b * P:2048 + (b + 1) * P],
                                                  prob[:, w % 2, b * P:(b + 1) * P], ident[:])
                            mm.then_inc(a_t, 1)
                        w = u - 2
                        if 0 <= w < U:
                            what, hh, n, s0 = todo[w]
                            blocks = (768 - s0) // P
                            pe.wait_ge(a_pt, ub + (w + 1))
                            pe.wait_ge(a_on, ub + w)
                            for b in range(5 - blocks, 5):
                                if kind == NA:
                                    v = VN[:, (8 + b - 3) if b >= 3 else 2 * n + (b - 1), bass.ds(p * P + hh * HD, HD)]
                                else:
                                    tile = LT + b - 3 if b >= 3 else max(n - 1, 0) + b - (5 - blocks)
                                    v = Vw[:, tile, bass.ds(g * HD, HD)]
                                mm = pe.matmul(PS[:, 6, 0:HD], probT[:, w % 2, b * P:(b + 1) * P], v,
                                               start=b == 5 - blocks, stop=b == 4)
                            mm.then_inc(a_o, 1)
                        w = u - 3
                        if w >= 0 and w % 2:
                            q = w // 2
                            pe.wait_ge(a_on, ub + (w + 1))
                            pe.wait_ge(a_oc, ob + q)
                            pe.transpose(PS[:, 7, 0:P], o_sb[:, q % 2, :], ident[:]).then_inc(a_ot, 1)

            def pool(l):
                groups = token_groups(l)
                ng = len(groups)

                def mix(g):
                    pe.wait_ge(p_pool, l * PAIRS + g + 1)
                    if g:
                        pe.wait_ge(p_ya, py_base[l] + ng * g)
                    for i, (t0, n) in enumerate(groups):
                        pe.matmul(PS[:, 4 + i, 0:n], wpool[:, g, :], pooled[:, t0:t0 + n], start=True, stop=True).then_inc(p_y, 1)

                pe.wait_ge(a_oc, (unit_base(l, SWA) + PAIRS * UN[l]) // 2)
                pe.wait_ge(p_in, 32 * (l + 1))
                for g in range(PAIRS):
                    pe.wait_ge(p_w[g % 2], 16 * (2 * l + g // 2 + 1))
                    if g >= 2:
                        pe.wait_ge(p_c, l * PAIRS + g - 1)
                    for i, (t0, n) in enumerate(groups):
                        for k in range(KB):
                            mm = pe.matmul(PS[:, 2 * (g % 2) + i, 0:n], wa[:, g % 2, k, :], hT[:, k, t0:t0 + n],
                                           start=k == 0, stop=k == KB - 1)
                    mm.then_inc(p_z, 1)
                    if g:
                        mix(g - 1)
                mix(PAIRS - 1)
                pe.wait_ge(p_ya, py_base[l + 1])

            def merge(l):
                groups = token_groups(l)
                base = 3 * KB * l
                with pe.Fori(0, KB // 2) as i:
                    for r in range(2):
                        pe.wait_ge(m_w[r], 16 * i + 16 * (l * KB // 2 + 1))
                        for b in range(3):
                            e = 3 * r + b
                            pe.wait_ge(m_m, 6 * i + (base + e + 1))
                            for s, (t0, n) in enumerate(groups):
                                for k in range(KB):
                                    mm = pe.matmul(PS[:, 4 * (e % 2) + s, 0:n], wgb[r][:, b * KB + k, :], hT[:, k, t0:t0 + n],
                                                   start=k == 0, stop=k == KB - 1)
                            mm.then_inc(m_z, 1)
                            for s, (t0, n) in enumerate(groups):
                                for k in range(PAIRS):
                                    mm = pe.matmul(PS[:, 4 * (e % 2) + 2 + s, 0:n], wgb[r][:, 3 * KB + b * PAIRS + k, :],
                                                   oT[b][:, k, t0:t0 + n], start=k == 0, stop=k == PAIRS - 1)
                            mm.then_inc(m_y, 1)

            def out_projection(l):
                pe.wait_ge(m_m, 2 + 3 * KB * (l + 1))
                pe.wait_ge(s_wo, 16 * (l + 1))
                for x in range(2 * live_tiles(l)):
                    k, half = x // 2, x % 2
                    if x >= 4:
                        pe.wait_ge(g_x, gx_base[l] + x - 3)
                    for kb in range(KB):
                        mm = pe.matmul(PS[:, x % 4, :], mT[:, kb, k * P:(k + 1) * P], wout[:, kb, half * 512:(half + 1) * 512],
                                       start=kb == 0, stop=kb == KB - 1)
                    mm.then_inc(g_z, 1)

            def queries(l):
                groups, nt = token_groups(l), live_tiles(l)
                ng = len(groups)
                pe.wait_ge(n_c, c_base[2 * l + 2])
                pe.wait_ge(g_x, gx_base[l + 1])
                with pe.Fori(0, HEADS) as i:
                    for r in range(2):
                        pe.wait_ge(q_w[r], 16 * i + 16 * (l * HEADS + 1))
                        for s, (t0, n) in enumerate(groups):
                            for k in range(KB):
                                mm = pe.matmul(PS[:, 4 * r + s, 0:n], wqs[:, r, k, :], hT[:, k, t0:t0 + n],
                                               start=k == 0, stop=k == KB - 1)
                            mm.then_inc(q_z, 1)
                        pe.wait_ge(q_sc, 2 * i + (2 * HEADS * l + r + 1))
                        for k in range(nt):
                            if k % LT == 0:
                                pe.wait_ge(q_c, 2 * ng * i + (qz_base[l] + r * ng + k // LT + 1))
                            mm = pe.matmul(PSF[:, 2048 * r + 1024 + k * P:2048 * r + 1024 + (k + 1) * P],
                                           qb[:, r, k * P:(k + 1) * P], wqs[:, r, KB, :], start=True, stop=True)
                        mm.then_inc(q_s, 1)

            def experts(l):
                pe.wait_ge(q_sc, 2 + 2 * HEADS * (l + 1))
                with pe.Fori(0, live_tiles(l)) as k:
                    with pe.Fori(0, HEADS // 2) as hp:
                        for e in range(2):
                            it = k * HEADS + hp * 2 + (it_base[l] + e)
                            pe.wait_ge(f_acc, it + 1)
                            for s in range(TOPK):
                                pe.wait_ge(f_dg, it * TOPK + (s + 1))
                                pe.wait_ge(g_v[s % RING], it * 32 + 16 * (s // RING + 1))
                                for half in range(2):
                                    mm = pe.matmul(PS[:, 2 * e + half, :], diag[:, s % 4, :],
                                                   V[:, s % RING, half * 512:(half + 1) * 512],
                                                   start=s == 0, stop=s == TOPK - 1)
                                mm.then_inc(v_free, 1)

            for l in range(DEPTH):
                norm(2 * l, NT)
                tokens(l)
                attention(l, NA)
                attention(l, SWA)
                pool(l)
                merge(l)
                out_projection(l)
                norm(2 * l + 1, live_tiles(l))
                queries(l)
                experts(l)

        @block.scalar
        def _(act):
            act.wait_ge(s_const, 16 * 7)
            act.activation(att[:, 0:4, :].rearrange("p a b -> p (a b)"), csil[:].rearrange("p k v -> p (k v)"),
                           ACT.Sigmoid).then_inc(s_sg, 1)
            with act.Fori(0, DEPTH * MCH // 2) as i:
                for r in range(2):
                    act.wait_ge(s_mod, 2 * i + (r + 2))
                    act.dma_start(t["mods_d"][2 * i + r], mout[0:2, r, :]).then_inc(s_mst[r], 16)

            def norm(i, tiles):
                act.wait_ge(n_ss, i + 1)
                act.activation(ss[:, 2, :], ss[:, 1, :], ACT.Sqrt).then_inc(n_sq, 1)
                for x in range(2 * tiles):
                    k, half = x // 2, x % 2
                    act.wait_ge(n_t, c_base[i] + x + 1)
                    act.activation(hT[:, 4 * half:4 * half + 4, k * P:(k + 1) * P],
                                   PS[:, x % 4, :].rearrange("p (b n) -> p b n", n=P), ACT.Copy).then_inc(n_c, 1)

            def tokens(l):
                nt = live_tiles(l)

                def turn(k):
                    cols = slice(k * P, (k + 1) * P)
                    act.wait_ge(s_bt, bt_base[l] + k + min(k, nt) + 1)
                    act.activation(kwT[:, :, cols], PS[:, 6, 0:2 * P].rearrange("p (g n) -> p g n", n=P), ACT.Copy).then_inc(s_bc, 1)
                    if k < nt:
                        act.wait_ge(s_bt, bt_base[l] + k + min(k, nt) + 2)
                        act.activation(qwT[:, :, cols], PS[:, 7, :].rearrange("p (g n) -> p g n", n=P), ACT.Copy).then_inc(s_bc, 1)

                for k in range(NT):
                    act.wait_ge(s_tz[0], l * NT + k + 1)
                    done = l * NT // 2 + k // 2
                    if k >= 2:
                        act.wait_ge(s_vout[k % 2], 16 * done)
                    act.activation(vn_st[:, k % 2, :], PS[:, 3 * (k % 2), :], ACT.Copy).then_inc(s_vst, 1)
                    if k:
                        turn(k - 1)
                turn(NT - 1)

            def attention(l, kind):
                U = UN[l]
                todo = units(l, kind)
                nq = SEQ if ZN[l] == 3 else TOK
                if kind == NA:
                    act.wait_ge(s_tz[2], q_base[l + 1])
                    act.wait_ge(s_bt, bt_base[l + 1])
                with pair_loop(act, kind) as (p, g):
                    if kind == NA:
                        for bank, (dst, t0, n) in enumerate(((k_st, 0, SEQ), (k_st, SEQ, CTX), (q_st, 0, SEQ), (q_st, SEQ, CTX))[:ZN[l]]):
                            act.wait_ge(a_z, z_base(l) + bank + 1 + p * ZN[l])
                            out, src = dst[:, t0:t0 + n], PS[:, bank, 0:n]
                            if bank == 2:
                                out = out.rearrange("p (n r c) -> p n r c", r=ROWS, c=QC)
                                src = src.rearrange("p (r n c) -> p n r c", n=NCB, c=QC)
                            act.activation(out, src, ACT.Copy).then_inc(a_zc, 1)
                    else:
                        act.activation(k_st, kwT[:, g, :], ACT.Copy).then_inc(a_sk, 1)
                        act.activation(q_st[:, 0:nq], qwT[:, p, 0:nq], ACT.Copy).then_inc(a_sk, 1)
                    ub = unit_base(l, kind) + p * U
                    ob = unit_base(l, kind) // 2 + p * (U // 2)
                    for u in range(U + 4):
                        if u < U:
                            what, hh, n, s0 = todo[u]
                            c = att[:, u % 4, :]
                            at = 1024 * (u % 2)
                            act.wait_ge(a_nm, ub + (u + 1))
                            if u >= 2:
                                act.wait_ge(a_t, ub + (u - 1))
                            ins = act.activation(prob[:, u % 2, s0 - P:640], PSF[:, at + s0:at + 768], ACT.Exp,
                                                 bias=c[:, 1:2], scale=SCALE, accum_out=c[:, 2:3])
                            if kind == SWA:
                                ins = act.activation(c[:, 3:4], sink_st[:, hh:hh + 1], ACT.Exp, bias=c[:, 1:2])
                            ins.then_inc(a_p, 1)
                        w = u - 1
                        if 0 <= w < U:
                            lo = todo[w][3] - P
                            act.wait_ge(a_t, ub + (w + 1))
                            if w >= 2:
                                act.wait_ge(a_o, ub + (w - 1))
                            act.activation(probT[:, w % 2, lo:640], PSF[:, 2048 + lo:2048 + 640], ACT.Copy).then_inc(a_pt, 1)
                        w = u - 3
                        if w >= 0 and w % 2:
                            q = w // 2
                            what, hh, n, s0 = todo[w]
                            act.wait_ge(a_ot, ob + (q + 1))
                            src = PS[:, 7, 0:P]
                            dst = q_tokens(kind, what, n)(oT[1 + kind][:, p, :])
                            if what == "lat" and kind == NA:
                                src = src.rearrange("p (r c) -> p r c", c=QC)
                            act.activation(dst, src, ACT.Copy).then_inc(a_oc, 1)

            def pool(l):
                groups = token_groups(l)
                ng = len(groups)

                def mix(g):
                    for i, (t0, n) in enumerate(groups):
                        act.wait_ge(p_y, py_base[l] + ng * g + i + 1)
                        act.activation(oT[0][:, g, t0:t0 + n], PS[:, 4 + i, 0:n], ACT.Copy, scale=pscale[:, g:g + 1]).then_inc(p_ya, 1)

                act.wait_ge(p_pad, l + 1)
                act.wait_ge(p_in, 32 * (l + 1))
                for g in range(PAIRS):
                    act.wait_ge(p_z, l * PAIRS + g + 1)
                    if g:
                        act.wait_ge(p_pool, l * PAIRS + g)
                    for i, (t0, n) in enumerate(groups):
                        o = PADL if i == 0 else 3 * PADL + SEQ
                        ins = act.activation(a_pad[:, o:o + n], PS[:, 2 * (g % 2) + i, 0:n], ACT.Copy)
                    ins.then_inc(p_c, 1)
                    if g:
                        mix(g - 1)
                mix(PAIRS - 1)

            def merge(l):
                n = live_tiles(l) * P
                base = 3 * KB * l
                with act.Fori(0, KB // 2) as i:
                    for e in range(6):
                        act.wait_ge(m_z, 6 * i + (base + e + 1))
                        act.wait_ge(m_m, 6 * i + (base + e + 1))
                        act.activation(sig[:, e % 2, 0:n], PSF[:, 2048 * (e % 2):2048 * (e % 2) + n], ACT.Sigmoid).then_inc(m_sig, 1)

            def queries(l):
                groups = token_groups(l)
                ng = len(groups)
                with act.Fori(0, HEADS) as i:
                    for r in range(2):
                        for s, (t0, n) in enumerate(groups):
                            act.wait_ge(q_z, 2 * ng * i + (qz_base[l] + r * ng + s + 1))
                            if s == 0:
                                act.wait_ge(q_sc, 2 * i + (2 * HEADS * l + r + 1))
                            act.activation(qb[:, r, t0:t0 + n], PS[:, 4 * r + s, 0:n], ACT.Copy).then_inc(q_c, 1)

            def experts(l):
                act.wait_ge(q_s, 2 * HEADS * (l + 1))

                def exps(n, e):
                    act.wait_ge(f_nm, n + (it_base[l] + 1))
                    act.activation(top_ex[:, e, :], best[:], ACT.Exp, bias=red[:, 0:1],
                                   accum_out=red[:, 1 + 2 * e:2 + 2 * e]).then_inc(f_ex, 1)

                def diagonals(n, e, slots):
                    act.wait_ge(f_w, n + (it_base[l] + 1))
                    for s in slots:
                        act.wait_ge(v_free, n * TOPK + (it_base[l] * TOPK + RING + s - 3))
                        act.activation(diag[:, s % 4, :], ident[:], ACT.Copy, scale=wgt[:, e, s:s + 1]).then_inc(f_dg, 1)

                def body(n, e, first, last):
                    if not first:
                        diagonals(n - 1, 1 - e, range(0, TOPK // 2))
                    if not last:
                        exps(n + 1, 1 - e)
                    if not first:
                        diagonals(n - 1, 1 - e, range(TOPK // 2, TOPK))
                    act.wait_ge(u_free, n * TOPK + (it_base[l] * TOPK + RING + TOPK))
                    act.activation(act_out[:, e, :], act_in[:, e, :], ACT.Gelu).then_inc(f_gel, 1)

                exps(0, 0)
                rounds(act, l, body)
                diagonals(HEADS * live_tiles(l) - 1, 1, range(TOPK))

            for l in range(DEPTH):
                norm(2 * l, NT)
                tokens(l)
                attention(l, NA)
                attention(l, SWA)
                pool(l)
                merge(l)
                norm(2 * l + 1, live_tiles(l))
                queries(l)
                experts(l)
            act.wait_ge(n_ss, norms)
            act.activation(ss[:, 2, :], ss[:, 1, :], ACT.Sqrt).then_inc(n_sq, 1)

        @block.vector
        def _(dve):
            step = Steps(dve, s_dve)
            dve.memset(red[:, 0:1], 0.0).then_inc(u_free, RING)
            dve.memset(red[:, 1:2], 0.0).then_inc(v_free, RING)
            dve.memset(red[:, 2:3], 0.0).then_inc(f_acc, 2)
            dve.memset(red[:, 3:4], 0.0).then_inc(m_m, 2)
            dve.memset(ss[:], 1.0).then_inc(q_sc, 2)
            dve.wait_ge(s_sg, 1)
            dve.tensor_tensor(csil[:], csil[:], att[:, 0:4, :].rearrange("p a (b v) -> p (a b) v", v=2), ALU.mult).then_inc(s_silu, 1)
            with step.loop(DEPTH * MCH // 2, 4) as i:
                for r in range(2):
                    dve.wait_ge(s_mz, 2 * i + (r + 1))
                    dve.wait_ge(s_mst[r], 16 * i + 1)
                    row = mout[0:2, r, :]
                    step.done(dve.tensor_tensor(row, PS[0:2, r, :], mrow[0:2, r, 0:512], ALU.add))
                    step.done(dve.tensor_tensor(row, row, mrow[0:2, r, 512:1024], ALU.add))
                    dve.tensor_tensor(row, row, mrow[0:2, r, 1024:1536], ALU.mult).then_inc(s_mod, 1)
            dve.wait_ge(s_x, 32)

            def rstd(i, tiles):
                for k in range(tiles):
                    ins = dve.tensor_tensor_reduce(H[:, k, :], X[:, k, :], X[:, k, :], 1.0, 0.0, ALU.mult, ALU.add, ss[:, 0, k:k + 1])
                step.done(ins)
                dve.tensor_scalar(ss[:, 1, :], ss[:, 0, :], 1.0 / D, EPS, ALU.mult, ALU.add).then_inc(n_ss, 1)
                dve.wait_ge(n_sq, i + 1)
                step.done(dve.reciprocal(ss[:, 0, :], ss[:, 2, :]))

            def norm(l, which, tiles):
                i = 2 * l + which
                rstd(i, tiles)
                dve.wait_ge(n_in[i], 16 * 12)
                for k in range(tiles):
                    v = 0 if k < LT else 1
                    step.done(dve.scalar_tensor_tensor(H[:, k, :], X[:, k, :], ss[:, 0, k:k + 1], modb[:, 2 * v + 1, :], ALU.mult, ALU.mult))
                    dve.tensor_tensor(H[:, k, :], H[:, k, :], modb[:, 2 * v, :], ALU.add).then_inc(n_h, 1)

            def rotate(dst, src, nh, k):
                heads = lambda ap: ap.rearrange("p (h d) -> p h d", d=HD)
                wide = lambda ap: ap.rearrange("p (h a s f) -> p h a s f", a=2, s=2, f=16)
                step.done(dve.tensor_tensor(heads(dst), heads(src), rope_cos[:, k, :].unsqueeze(1).to_broadcast([P, nh, HD]), ALU.mult))
                tmp = r_tmp[:, 0:nh * HD]
                sin = rope_sin[:, k, :].rearrange("p (a s f) -> p a s f", s=2, f=16)
                for s in range(2):
                    step.done(dve.tensor_tensor(wide(tmp)[:, :, :, s, :], wide(src)[:, :, :, 1 - s, :],
                                                sin[:, :, s, :].unsqueeze(1).to_broadcast([P, nh, 2, 16]), ALU.mult))
                return dve.tensor_tensor(dst, dst, tmp, ALU.add)

            def tokens(l):
                nt = live_tiles(l)
                for k in range(NT):
                    if k >= 2:
                        dve.wait_ge(s_bt, bt_base[l] + (k - 1) + min(k - 1, nt))
                    kd = kdup[:, k % 2, :].rearrange("p (g u d) -> p g u d", u=2, d=HD)
                    dve.wait_ge(s_tz[1], l * NT + k + 1)
                    if k:
                        dve.wait_ge(s_kd, l * NT + k)
                    dve.tensor_copy(Vw[:, k, :], PS[:, 3 * (k % 2) + 1, P:2 * P])
                    src = PS[:, 3 * (k % 2) + 1, 0:P]
                    if k < LT:
                        step.done(rotate(k_rot, src, 2, k))
                    else:
                        step.done(dve.tensor_copy(k_rot, src))
                    for u in range(2):
                        ins = dve.tensor_copy(kd[:, :, u, :], k_rot.rearrange("p (g d) -> p g d", d=HD))
                    ins.then_inc(s_kd, 1)
                    if k < nt:
                        dve.wait_ge(s_tz[2], q_base[l] + k + 1)
                        src = PS[:, 3 * (k % 2) + 2, :]
                        if k < LT:
                            ins = rotate(q_rot[:, k % 2, :], src, HEADS, k)
                        else:
                            ins = dve.tensor_copy(q_rot[:, k % 2, :], src)
                        ins.then_inc(s_qd, 1)

            def softmax_bias(kind, todo, u, p):
                what, hh, n, s0 = todo[u]
                at = 1024 * (u % 2)
                if what == "ctx":
                    return 0
                if kind == NA:
                    s = PSF[:, at + s0:at + 512].rearrange("p (r c) -> p r c", c=KC)
                    w0 = key_start(n) - n * QC + 16
                    step.done(dve.scalar_tensor_tensor(s, rpbT[:, p * 2 + hh, :, w0:w0 + KC], 1.0 / SCALE, s, ALU.mult, ALU.add))
                    step.done(dve.tensor_tensor(s, s, na_mask[:, n, :].unsqueeze(1).to_broadcast([P, ROWS, KC]), ALU.add))
                    return 2
                steps = 0
                for side, there, lo in ((0, n > 0, s0), (1, n < LT - 1, 512 - P)):
                    if there:
                        s = PSF[:, at + lo:at + lo + P]
                        step.done(dve.tensor_tensor(s, s, swa_mask[:, side, :], ALU.add))
                        steps += 1
                return steps

            def attention(l, kind):
                U = UN[l]
                todo = units(l, kind)
                lat = 2 * NCB
                per = (2 * lat if kind == NA else 2 * 2 * (NCB - 1)) + U * (1 if kind == NA else 2) + U * (1 if kind == NA else 2) + (0 if kind == NA else 1)
                if kind == NA:
                    dve.wait_ge(s_rpb[l], 16)
                else:
                    dve.wait_ge(s_sink[l], 16)
                with pair_loop(dve, kind, step, per) as (p, g):
                    ub = unit_base(l, kind) + p * U
                    ob = unit_base(l, kind) // 2 + p * (U // 2)
                    if kind == SWA:
                        step.done(dve.tensor_copy(sink_st[:], sinks[:, bass.ds(p * 2, 2)]))
                    for u in range(U + 2):
                        if u < U:
                            what, hh, n, s0 = todo[u]
                            at = 1024 * (u % 2)
                            c = att[:, u % 4, :]
                            dve.wait_ge(a_s, ub + (u + 1))
                            softmax_bias(kind, todo, u, p)
                            step.done(dve.tensor_reduce(c[:, 0:1], PSF[:, at + s0:at + 768], AX.X, ALU.max))
                            if kind == SWA:
                                step.done(dve.tensor_scalar(c[:, 0:1], c[:, 0:1], SCALE, sink_st[:, hh:hh + 1], ALU.mult, ALU.max))
                                dve.tensor_scalar(c[:, 1:2], c[:, 0:1], -1.0, None, ALU.mult).then_inc(a_nm, 1)
                            else:
                                dve.tensor_scalar(c[:, 1:2], c[:, 0:1], -SCALE, None, ALU.mult).then_inc(a_nm, 1)
                        w = u - 1
                        if 0 <= w < U:
                            c = att[:, w % 4, :]
                            dve.wait_ge(a_p, ub + (w + 1))
                            if kind == SWA:
                                step.done(dve.tensor_tensor(c[:, 2:3], c[:, 2:3], c[:, 3:4], ALU.add))
                            step.done(dve.reciprocal(c[:, 0:1], c[:, 2:3]))
                        w = u - 2
                        if 0 <= w < U:
                            what, hh, n, s0 = todo[w]
                            q = w // 2
                            dve.wait_ge(a_o, ub + (w + 1))
                            if q >= 2:
                                dve.wait_ge(a_ot, ob + (q - 1))
                            dve.tensor_scalar(o_sb[:, q % 2, hh * HD:(hh + 1) * HD], PS[:, 6, 0:HD],
                                              att[:, w % 4, 0:1], None, ALU.mult).then_inc(a_on, 1)

            def pool(l):
                groups = token_groups(l)
                dve.memset(a_pad, 0.0).then_inc(p_pad, 1)
                for g, w in enumerate(POOLS):
                    dve.wait_ge(p_c, l * PAIRS + g + 1)
                    dve.wait_ge(p_inv, 16 * (l * PAIRS + g + 1))
                    if g:
                        dve.wait_ge(p_y, py_base[l] + len(groups) * g)
                    src, length, have = a_pad, PADW, 1
                    while have < w:
                        dst = win[:, have.bit_length() % 2, :]
                        length -= have
                        step.done(dve.tensor_tensor(dst[:, 0:length], src[:, 0:length], src[:, have:have + length], ALU.add))
                        src, have = dst, 2 * have
                    for i, (t0, n) in enumerate(groups):
                        o = PADL if i == 0 else 3 * PADL + SEQ
                        step.done(dve.tensor_tensor(pooled[:, t0:t0 + n], src[:, o - w // 2:o - w // 2 + n], inv_n[:, t0:t0 + n], ALU.mult))
                        ins = dve.tensor_tensor(pooled[:, t0:t0 + n], pooled[:, t0:t0 + n], a_pad[:, o:o + n], ALU.subtract)
                    ins.then_inc(p_pool, 1)

            def merge(l):
                n = live_tiles(l) * P
                base = 3 * KB * l
                with step.loop(KB // 2, 4) as i:
                    for r in range(2):
                        for b in range(3):
                            e = 3 * r + b
                            gate_b, y = sig[:, e % 2, 0:n], PSF[:, 2048 * (e % 2) + 1024:2048 * (e % 2) + 1024 + n]
                            row = mT[:, 2 * i + r, 0:n]
                            dve.wait_ge(m_sig, 6 * i + (base + e + 1))
                            dve.wait_ge(m_y, 6 * i + (base + e + 1))
                            if b == 0:
                                dve.tensor_tensor(row, gate_b, y, ALU.mult).then_inc(m_m, 1)
                            else:
                                dve.wait_ge(m_m, 6 * i + (base + e + 2))
                                step.done(dve.tensor_tensor(mtmp[:, 0:n], gate_b, y, ALU.mult))
                                dve.tensor_tensor(row, row, mtmp[:, 0:n], ALU.add).then_inc(m_m, 1)

            def out_projection(l):
                for x in range(2 * live_tiles(l)):
                    k, half = x // 2, x % 2
                    cols = slice(half * 512, (half + 1) * 512)
                    dve.wait_ge(g_z, gx_base[l] + x + 1)
                    if x == 0:
                        dve.wait_ge(m_m, 2 + 3 * KB * (l + 1))
                    if x >= 2:
                        dve.wait_ge(g_x, gx_base[l] + x - 1)
                    step.done(dve.tensor_tensor(xtmp[:, half, :], PS[:, x % 4, :], gt[:, 0 if k < LT else 1, cols], ALU.mult))
                    dve.tensor_tensor(X[:, k, cols], X[:, k, cols], xtmp[:, half, :], ALU.add).then_inc(g_x, 1)
                dve.wait_ge(g_x, gx_base[l + 1])

            def queries(l):
                nt = live_tiles(l)
                table = S_all[:, 0:NT * 2 * HEADS * P].rearrange("p (k b n) -> p k b n", k=NT, n=P)
                with dve.Fori(0, HEADS) as i:
                    for r in range(2):
                        dve.wait_ge(q_s, 2 * i + (2 * HEADS * l + r + 1))
                        dve.tensor_copy(table[:, 0:nt, 2 * i + r, :],
                                        PSF[:, 2048 * r + 1024:2048 * r + 1024 + nt * P].rearrange("p (k n) -> p k n", n=P)).then_inc(q_sc, 1)
                dve.wait_ge(q_sc, 2 + 2 * HEADS * (l + 1))

            def top16(values, indices, rows, cut):
                step.done(dve.max(values[:, 0:8], rows), s_held)
                dve.max_index(indices[:, 0:8], values[:, 0:8], rows)
                step.done(dve.match_replace(cut, values[:, 0:8], rows, LOW), s_held)
                step.done(dve.max(values[:, 8:16], cut), s_held)
                return dve.max_index(indices[:, 8:16], values[:, 8:16], cut)

            def route(n, e, l):
                step.done(dve.tensor_copy(s_st.rearrange("p a n -> p (a n)"), S_all[:, bass.ds(n * (2 * P), 2 * P)]), s_held)
                for side in range(2):
                    ins = top16(v16[:, side, :], i16[:, side, :], s_st[:, side, :], s_cut[:, side, :])
                    step.done(ins, s_held)
                dve.tensor_scalar(code[:, 0:TOPK], i16[:, 0, :], float(NKEYS), None, ALU.mult)
                step.done(dve.tensor_copy(code[:, TOPK:2 * TOPK], i16[:, 1, :]))
                step.done(dve.tensor_tensor(cand, v16[:, 0, :].unsqueeze(2).to_broadcast([P, TOPK, TOPK]),
                                            v16[:, 1, :].unsqueeze(1).to_broadcast([P, TOPK, TOPK]), ALU.add), s_held)
                flat = cand.rearrange("p a b -> p (a b)")
                if not (isinstance(n, int) and n == 0):
                    dve.wait_ge(f_ex, n + it_base[l])
                    dve.sem_inc(s_held, 1)
                step.done(top16(best, best_j, flat, cand_cut.rearrange("p a b -> p (a b)")))
                dve.tensor_scalar(red[:, 0:1], best[:, 0:1], -1.0, None, ALU.mult).then_inc(f_nm, 1)
                step.done(dve.tensor_scalar(ab_u[:, :, 0], best_j[:], 4, None, ALU.logical_shift_right))
                step.done(dve.tensor_scalar(ab_u[:, :, 1], best_j[:], 15, None, ALU.bitwise_and))
                step.done(dve.tensor_copy(ab[:], ab_u[:]))
                oh = onehot.rearrange("p k (s j) -> p k s j", s=2)
                step.done(dve.tensor_tensor(oh, ab[:].unsqueeze(3).to_broadcast([P, TOPK, 2, TOPK]),
                                            iota[:].unsqueeze(1).unsqueeze(1).to_broadcast([P, TOPK, 2, TOPK]), ALU.is_equal))
                step.done(dve.tensor_tensor(onehot, onehot, code[:].unsqueeze(1).to_broadcast([P, TOPK, 2 * TOPK]), ALU.mult))
                step.done(dve.tensor_reduce(expert_f[:], onehot, AX.X, ALU.add))
                dve.tensor_copy(expert_u[:, e, :], expert_f[:]).then_inc(f_idx, 1)

            def experts(l):
                base = it_base[l]

                def products(n, e, slots):
                    for s in slots:
                        dve.wait_ge(g_u[s % RING], n * 32 + (base * 32 + 16 * (s // RING + 1)))
                        row = U[:, s % RING, :]
                        dve.tensor_tensor_reduce(row, row, h_st, 1.0, 0.0, ALU.mult, ALU.add,
                                                 act_in[:, e, s:s + 1]).then_inc(u_free, 1)

                def update(n, e):
                    tile = n // HEADS
                    v = 0 if l == DEPTH - 1 else tile // LT
                    row = X[:, tile, :]
                    dve.wait_ge(v_free, n * TOPK + (base * TOPK + RING + TOPK))
                    dve.tensor_tensor(x_upd, PSF[:, 1024 * e:1024 * (e + 1)], gt[:, v, :], ALU.mult).then_inc(f_acc, 1)
                    dve.wait_ge(f_acc, n + (base + 3))
                    step.done(dve.tensor_tensor(row, row, x_upd, ALU.add))

                def body(n, e, first, last):
                    step.done(dve.tensor_copy(h_st, H[:, n // HEADS, :]))
                    dve.tensor_copy(expert_v[:, e, :], expert_u[:, e, :]).then_inc(f_vidx, 1)
                    products(n, e, range(0, 4))
                    if not last:
                        route(n + 1, 1 - e, l)
                    products(n, e, range(4, TOPK))
                    dve.wait_ge(f_ex, n + (base + 1))
                    step.done(dve.reciprocal(red[:, 2:3], red[:, 1 + 2 * e:2 + 2 * e]))
                    step.done(dve.tensor_scalar(gate[:, e, :], top_ex[:, e, :], red[:, 2:3], None, ALU.mult))
                    dve.wait_ge(f_gel, n + (base + 1))
                    dve.tensor_tensor(wgt[:, e, :], gate[:, e, :], act_out[:, e, :], ALU.mult).then_inc(f_w, 1)
                    if not first:
                        update(n - 1, 1 - e)

                first = step.n
                route(0, 0, l)
                rounds(dve, l, body, step, step.n - first + 4)
                update(HEADS * live_tiles(l) - 1, 1)

            for l in range(DEPTH):
                norm(l, 0, NT)
                tokens(l)
                attention(l, NA)
                attention(l, SWA)
                pool(l)
                merge(l)
                out_projection(l)
                norm(l, 1, live_tiles(l))
                queries(l)
                experts(l)
            rstd(2 * DEPTH, LT)
            dve.wait_ge(n_in[2 * DEPTH], 16)
            for k in range(LT):
                dve.scalar_tensor_tensor(H[:, k, :], X[:, k, :], ss[:, 0, k:k + 1], modb[:, 0, :], ALU.mult, ALU.mult).then_inc(n_h, 1)

        @block.gpsimd
        def _(pool):
            for l in range(DEPTH):
                base = it_base[l]
                pool.wait_ge(q_s, 2 * HEADS * (l + 1))

                def gather(ring, table, places, free, landed, n, s):
                    pool.wait_ge(free, n * TOPK + (base * TOPK + s + 1))
                    if not isinstance(n, int):
                        pool.sem_inc(s_held, 1)
                    pool.indirect_dma_start(ring[:, s % RING, :], None, table, bass.IndirectOffsetOnAxis(
                        ap=places[:, s:s + 1], axis=0)).then_inc(landed[s % RING], 16)

                def body(n, e, first, last):
                    pool.wait_ge(f_idx, n + (base + 1))
                    if not first:
                        pool.wait_ge(f_vidx, n + base)
                    for s in range(TOPK):
                        gather(U, t["peer_u"][l], expert_u[:, e, :], u_free, g_u, n, s)
                        if not first:
                            gather(V, t["peer_v"][l], expert_v[:, 1 - e, :], v_free, g_v, n - 1, s)

                rounds(pool, l, body)
                n = HEADS * live_tiles(l)
                pool.wait_ge(f_vidx, n + base)
                for s in range(TOPK):
                    gather(V, t["peer_v"][l], expert_v[:, 1, :], v_free, g_v, n - 1, s)


def constants(np):
    inv = 10000.0 ** (-np.arange(16, dtype=np.float32) / np.float32(16))
    tok = np.arange(SEQ)
    ang = np.stack([(tok // GRID_W).astype(np.float32), (tok % GRID_W).astype(np.float32)], 1)[:, :, None] * inv.astype(np.float32)
    cos, sin = np.cos(ang), np.sin(ang)
    tiles = lambda a: np.ascontiguousarray(a.reshape(LT, P, HD).transpose(1, 0, 2).astype(np.float32))
    q = np.arange(P) % QC
    mask = np.full((P, NCB, KC), MASKED, np.float32)
    for n in range(NCB):
        start = np.clip(n * QC + q - 8, 0, GRID_W - 16)[:, None]
        col = key_start(n) + np.arange(KC)[None, :]
        mask[:, n, :][(col >= start) & (col < start + 16)] = 0.0
    i, j = np.arange(P)[:, None], np.arange(P)[None, :]
    swa = np.stack([np.where(j >= i, 0.0, MASKED), np.where(j <= i, 0.0, MASKED)], 1).astype(np.float32)
    inv_n = np.zeros((PAIRS, TOK), np.float32)
    for g, w in enumerate(POOLS):
        for t0, n in ((0, SEQ), (SEQ, CTX)):
            x = np.arange(n)
            inv_n[g, t0:t0 + n] = 1.0 / (np.clip(x - w // 2 + w, 0, n) - np.clip(x - w // 2, 0, n))
    return {
        "ident": np.eye(P, dtype=np.float32),
        "rope_cos": tiles(np.stack([cos, cos], 2)), "rope_sin": tiles(np.stack([-sin, sin], 2)),
        "na_mask": mask, "swa_mask": swa, "inv_n": inv_n,
        "iota": np.tile(np.arange(TOPK, dtype=np.float32), (P, 1)),
    }


def layouts(np, i):
    c = np.ascontiguousarray
    blocks = lambda w: w.reshape(KB, P, -1).transpose(1, 0, 2)
    w_in = i["w_in"]
    VNc, KWc, QNc, QWc, Ac, Gc = 512, 1024, 1280, 1792, 2304, 2816
    out = {"x": i["x"], "ctx": i["ctx"], "final_g": i["final_g"], "sink": i["swa_sink"]}
    out["cc"] = c(np.stack([i["c"][0], i["c_ctx"]]).reshape(2, KB, P).transpose(2, 1, 0))
    out["ada"] = c(i["ada_w"].reshape(DEPTH, KB, P, MCH, 512).transpose(0, 3, 2, 1, 4).reshape(DEPTH * MCH, P, KB, 512))
    one = np.ones((D,), np.float32)
    rows = []
    for l in range(DEPTH):
        add = np.concatenate([0 * one, one, 0 * one] * 2)
        gain = np.concatenate([one, i["norm1_g"][l], one, one, i["norm2_g"][l], one])
        r = np.stack([i["ada_b"][l], add, gain]).reshape(3, MCH, 512).transpose(1, 0, 2).reshape(MCH, 1, 1536)
        rows.append(np.repeat(r, 2, 1))
    out["mrow"] = c(np.concatenate(rows))
    out["w_tok"] = c(np.stack([np.concatenate(
        [blocks(w[:, a:a + n]).reshape(P, -1) for a, n in ((VNc, 512), (KWc, 256), (QWc, 512))], 1) for w in w_in]))
    out["wqk"] = c(np.stack([np.stack([blocks(w[:, QNc + p * P:QNc + (p + 1) * P]), blocks(w[:, p * P:(p + 1) * P])], 1)
                             for w in w_in for p in range(PAIRS)]))
    out["wa"] = c(np.stack([[blocks(w[:, Ac + g * P:Ac + (g + 1) * P]) for g in range(PAIRS)] for w in w_in]))
    out["pool_w"] = c(i["pool_w"].transpose(0, 2, 1, 3))
    out["pool_scale"] = c(i["pool_scale"].reshape(DEPTH, PAIRS, P).transpose(0, 2, 1))
    wide = np.zeros((DEPTH, 8, 15, 64), np.float32)
    wide[..., 16:47] = i["na_rpb"]
    r, q = np.arange(P)[:, None, None] // QC, np.arange(P)[:, None, None] % QC
    kr, w = np.arange(ROWS)[None, :, None], np.arange(TW)[None, None, :]
    out["rpb"] = c(wide[:, :, kr - r + ROWS - 1, w - q + 15].transpose(0, 2, 1, 3, 4))
    gb = []
    for l in range(DEPTH):
        for j in range(KB):
            cols = slice(j * P, (j + 1) * P)
            gates = [blocks(w_in[l][:, Gc + b * D + j * P:Gc + b * D + (j + 1) * P]) for b in range(3)]
            outs = [i[f"w_branch_{b}"][l][:, cols].reshape(PAIRS, P, P).transpose(1, 0, 2) for b in "abc"]
            gb.append(np.concatenate(gates + outs, 1))
    out["wgb"] = c(np.stack(gb))
    out["w_out"] = c(np.stack([blocks(w) for w in i["w_out"]]))
    out["wqs"] = c(np.stack([np.concatenate(
        [blocks(i["peer_wq"][l][:, b * P:(b + 1) * P]), i["peer_keys"][l, b // 2, b % 2].T[:, None, :]], 1)
        for l in range(DEPTH) for b in range(2 * HEADS)]))
    for l in range(DEPTH):
        out[f"peer_u{l}"] = c(i["peer_u"][l])
        out[f"peer_v{l}"] = c(i["peer_v"][l])
    return out


def kernel(**inputs):
    import numpy as np
    import concourse.bacc as bacc
    from concourse.bass_utils import run_bass_kernel_spmd as run

    arrays = layouts(np, {k: np.asarray(v) for k, v in inputs.items()}) | constants(np)
    nc = bacc.Bacc("TRN2", target_bir_lowering=False, num_devices=1)
    t = {k: nc.dram_tensor("in_" + k, a.shape, mybir.dt.from_np(a.dtype), kind="ExternalInput").ap() for k, a in arrays.items()}
    t["mods_d"] = nc.dram_tensor("mods_d", (DEPTH * MCH, 2, 512), F32).ap()
    t["vn_d"] = nc.dram_tensor("vn_d", (DEPTH, TOK, 512), F32).ap()
    t["out"] = nc.dram_tensor("out_0", (1, SEQ, D), F32, kind="ExternalOutput").ap()
    for name in ("peer_u", "peer_v"):
        t[name] = [t[f"{name}{l}"] for l in range(DEPTH)]
    build(nc, t)
    r = run(nc, [{"in_" + k: a for k, a in arrays.items()}], core_ids=[0])
    return r.results[0]["out_0"]
```

```python
from contextlib import ExitStack, contextmanager

import concourse.bass as bass
from concourse import mybir

F32 = mybir.dt.float32
U32 = mybir.dt.uint32
ALU = mybir.AluOpType
ACT = mybir.ActivationFunctionType
AX = mybir.AxisListType

P = 128
D = 1024
KB = D // P
DEPTH = 2
SEQ, CTX = 512, 256
TOK = SEQ + CTX
LT, CT = SEQ // P, CTX // P
NT = LT + CT
GRID_W, QC, KC = 64, 16, 32
ROWS = SEQ // GRID_W
NCB = GRID_W // QC
HD = 64
PAIRS = 4
TW = 48
MODS = 6 * D
MCH = MODS // 512
AR = 4
POOLS = (2, 4, 8, 16)
PADL = 8
PADW = PADL + SEQ + PADL + PADL + CTX + PADL
HEADS, TOPK, NKEYS = 8, 16, 128
RING = 8
SCALE = HD ** -0.5
EPS = 1e-6
LOW = -3.0e38
MASKED = -1.0e30
DB = KB // 2


def live_tiles(l):
    return NT if l < DEPTH - 1 else LT


def token_groups(l):
    return [(0, SEQ), (SEQ, CTX)] if l < DEPTH - 1 else [(0, SEQ)]


def key_start(n):
    return min(max(n * QC - 8, 0), GRID_W - KC)


class Steps:

    def __init__(self, eng, sem):
        self.eng, self.sem, self.n, self.at = eng, sem, 0, 0

    def done(self, instruction, held=None):
        instruction.then_inc(self.sem, 1)
        self.n += 1
        self.eng.wait_ge(self.sem, self.at + self.n)
        if held:
            self.eng.sem_inc(held, 1)

    @contextmanager
    def loop(self, count, per):
        first, outer = self.n, self.at
        with self.eng.Fori(0, count) as i:
            self.at = outer + i * per
            yield i
            assert self.n - first == per, f"the loop takes {self.n - first} steps"
        self.at = outer
        self.n = first + count * per


def build(nc, t):
    with ExitStack() as ctx:
        sb = lambda name, shape, dt=F32: ctx.enter_context(nc.sbuf_tensor(name, shape, dt))
        sem = lambda name: ctx.enter_context(nc.semaphore(name))
        per_layer = lambda name: [sem(f"{name}{l}") for l in range(DEPTH)]

        X = sb("X", [P, NT, D])
        H = sb("H", [P, NT, D])
        arena = sb("arena", [P, 33280])
        modb = sb("modb", [P, 4, D])
        gt = sb("gt", [P, 2, D])
        ident = sb("ident", [P, P])
        rope_cos = sb("rope_cos", [P, LT, HD])
        rope_sin = sb("rope_sin", [P, LT, HD])
        na_mask = sb("na_mask", [P, NCB, KC])
        swa_mask = sb("swa_mask", [P, 2, P])
        iota = sb("iota", [P, TOPK])
        sinks = sb("sinks", [P, 8])
        sink_st = sb("sink_st", [P, 4])
        ss = sb("ss", [P, 3, 8])
        att = sb("att", [P, 8, 4])
        csil = sb("csil", [P, KB, 2])
        PS = ctx.enter_context(nc.psum_tensor("PS", [P, 8, 512], F32))
        PSF = PS[:].rearrange("p b n -> p (b n)")

        def view(at, *dims):
            n = 1
            for d in dims:
                n *= d
            v = arena[:, at:at + n]
            if len(dims) == 2:
                return v.rearrange("p (a b) -> p a b", b=dims[1])
            if len(dims) == 3:
                return v.rearrange("p (a b c) -> p a b c", b=dims[1], c=dims[2])
            return v

        hT = view(27136, KB, TOK)
        qwT = view(0, PAIRS, TOK)
        kwT = view(3072, 2, TOK)
        Vw = view(4608, NT, P)
        VN = view(5376, 10, 512)
        oT = [view(10496 + 3072 * b, PAIRS, TOK) for b in range(3)]
        w_tok = view(10496, 10240)
        vn_st = view(20736, 2, 512)
        kdup = view(21760, 2, 2 * P)
        q_rot = view(22272, 2, 512)
        r_tmp = view(23296, 512)
        k_rot = view(23808, P)
        wqk_first = view(24576, 2, KB, P)
        wqk = view(19712, 2, KB, P)
        k_st = view(21760, TOK)
        q_st = view(22528, TOK)
        prob = view(23296, 2, 640)
        probT = view(24576, 2, 5 * P)
        v_st = view(25856, 10, P)
        vw_st = view(5376, NT, P)
        q_2nd = view(26112, TOK)
        rpbT = H[:].rearrange("p a b -> p (a b)")[:, 0:8 * ROWS * TW].rearrange(
            "p (h r w) -> p h r w", h=8, r=ROWS)
        a_pad = view(5376, PADW)
        win = view(6176, 2, PADW)
        inv_n = view(7776, TOK)
        pooled = view(8544, TOK)
        wa = view(19712, 2, KB, P)
        wpool = view(9312, PAIRS, P)
        pscale = view(9824, PAIRS)
        mT = view(0, KB, TOK)
        sig = view(6144, 2, TOK)
        mtmp = view(7680, TOK)
        wgb = [H[:].rearrange("p a b -> p (a b)")[:, 0:36 * P].rearrange("p (a b) -> p a b", b=P), view(19712, 36, P)]
        wout_l = [view(8448, DB, 512), view(24320, DB, 512)]
        wout_r = [view(10496, DB, 512), view(12544, DB, 512)]
        xtmp = view(14592, 2, 512)
        S_all = view(0, 12544)
        wqs = view(16384, 2, 9, P)
        qb = view(14848, 2, TOK)
        U = view(12544, RING, D)
        V = view(12544 + RING * D, RING, D)
        at = 12544 + 2 * RING * D
        h_st = view(at, D)
        x_upd = view(at + 1024, D)
        diag = view(at + 2048, 4, P)
        s_st = view(at + 2560, 2, P)
        s_cut = view(at + 2816, 2, P)
        cand = view(at + 3072, 16, 16)
        cand_cut = view(at + 3328, 16, 16)
        onehot = view(at + 3584, 16, 32)
        assert at + 4256 <= 33280
        v16 = sb("v16", [P, 2, TOPK])
        i16 = sb("i16", [P, 2, TOPK], U32)
        code = sb("code", [P, 2 * TOPK])
        best = sb("best", [P, TOPK])
        best_j = sb("best_j", [P, TOPK], U32)
        ab_u = sb("ab_u", [P, TOPK, 2], U32)
        ab = sb("ab", [P, TOPK, 2])
        expert_f = sb("expert_f", [P, TOPK])
        expert_u = sb("expert_u", [P, 2, TOPK], U32)
        expert_v = sb("expert_v", [P, 2, TOPK], U32)
        top_ex = view(at + 4160, 2, TOPK)
        gate = view(at + 4192, 2, TOPK)
        act_in = view(at + 4224, 2, TOPK)
        act_out = view(at + 4096, 2, TOPK)
        wgt = view(at + 4128, 2, TOPK)
        red = sb("red", [P, 4])
        ada = [view(4096 * r, KB, 512) for r in range(AR)]
        mrow = view(4096 * AR, AR, 3 * 512)
        mout = view((4096 + 1536) * AR, AR, 512)

        s_cc, s_const, s_x = sem("s_cc"), sem("s_const"), sem("s_x")
        s_dve = sem("s_dve")
        s_ada = [sem(f"s_ada{r}") for r in range(AR)]
        s_sg, s_silu = sem("s_sg"), sem("s_silu")
        s_mz, s_mod = sem("s_mz"), sem("s_mod")
        s_mst = [sem(f"s_mst{r}") for r in range(AR)]
        norms = 2 * DEPTH + 1
        n_in = [sem(f"n_in{i}") for i in range(norms)]
        n_ss, n_sq = sem("n_ss"), sem("n_sq")
        n_h, n_t, n_c = sem("n_h"), sem("n_t"), sem("n_c")
        s_wt = [[sem(f"s_wt{l}{c}") for c in range(3)] for l in range(DEPTH)]
        s_tz = [sem(f"s_tz{c}") for c in range(3)]
        s_vst, s_kd, s_qd, s_bt, s_bc = [sem(x) for x in ("s_vst", "s_kd", "s_qd", "s_bt", "s_bc")]
        s_vout = [sem(f"s_vout{r}") for r in range(2)]
        s_vn, s_rpb, s_sink = per_layer("s_vn"), per_layer("s_rpb"), per_layer("s_sink")
        s_wqk = sem("s_wqk")
        a_z, a_zc, a_sk = sem("a_z"), sem("a_zc"), sem("a_sk")
        a_s, a_nm, a_p, a_n, a_t, a_pt, a_v, a_o, a_oc = [
            sem(x) for x in ("a_s", "a_nm", "a_p", "a_n", "a_t", "a_pt", "a_v", "a_o", "a_oc")]
        p_w, p_in, p_inv = [sem("p_w0"), sem("p_w1")], sem("p_in"), sem("p_inv")
        p_pad, p_z, p_c, p_pool, p_y, p_ya = [sem(x) for x in ("p_pad", "p_z", "p_c", "p_pool", "p_y", "p_ya")]
        m_w = [sem("m_w0"), sem("m_w1")]
        m_z, m_y, m_sig, m_m = sem("m_z"), sem("m_y"), sem("m_sig"), sem("m_m")
        s_wo, g_z, g_x, s_gt = [sem("s_wo0"), sem("s_wo1")], sem("g_z"), sem("g_x"), sem("s_gt")
        q_w = [sem("q_w0"), sem("q_w1")]
        q_z, q_c, q_s, q_sc = sem("q_z"), sem("q_c"), sem("q_s"), sem("q_sc")
        g_u = [sem(f"g_u{r}") for r in range(RING)]
        g_v = [sem(f"g_v{r}") for r in range(RING)]
        u_free, v_free = sem("u_free"), sem("v_free")
        f_idx, f_vidx, f_nm, f_ex, f_gel, f_w, f_dg, f_acc = [
            sem(x) for x in ("f_idx", "f_vidx", "f_nm", "f_ex", "f_gel", "f_w", "f_dg", "f_acc")]
        s_store = sem("s_store")
        s_held = sem("s_held")

        def before(l, per):
            return sum(per(m) for m in range(l))

        NORM_TILES = [n for l in range(DEPTH) for n in (NT, live_tiles(l))] + [LT]
        HT_TILES = NORM_TILES[:-1] + [0]
        n_base = [sum(NORM_TILES[:i]) for i in range(norms + 1)]
        c_base = [2 * sum(HT_TILES[:i]) for i in range(norms + 1)]
        ngr = lambda l: len(token_groups(l))
        bt_count = lambda l: NT + live_tiles(l)
        q_base = [before(l, live_tiles) for l in range(DEPTH + 1)]
        bt_base = [before(l, bt_count) for l in range(DEPTH + 1)]
        py_base = [before(l, lambda m: PAIRS * ngr(m)) for l in range(DEPTH + 1)]
        gx_base = [before(l, lambda m: 2 * live_tiles(m)) for l in range(DEPTH + 1)]
        qz_base = [before(l, lambda m: 2 * HEADS * ngr(m)) for l in range(DEPTH + 1)]
        it_base = [before(l, lambda m: HEADS * live_tiles(m)) for l in range(DEPTH + 1)]

        NA, SWA = 0, 1

        def units(l, kind):
            out = []
            for n in range(NCB):
                for hh in range(2):
                    if kind == NA:
                        out.append(("lat", hh, n, 512 - 2 * P))
                    else:
                        blocks = min(n + 2, LT) - max(n - 1, 0)
                        out.append(("lat", hh, n, 512 - blocks * P))
            if l < DEPTH - 1:
                for n in range(CT):
                    for hh in range(2):
                        out.append(("ctx", hh, n, 512))
            return out

        UN = [len(units(l, NA)) for l in range(DEPTH)]
        ZN = [4, 3]

        def unit_base(l, kind):
            return 2 + sum(2 * PAIRS * UN[m] for m in range(l)) + kind * PAIRS * UN[l]

        def z_base(l):
            return 1 + sum(PAIRS * ZN[m] for m in range(l))

        def q_tokens(kind, what, n):
            if what == "ctx":
                return lambda ap: ap[:, SEQ + n * P:SEQ + (n + 1) * P]
            if kind == SWA:
                return lambda ap: ap[:, n * P:(n + 1) * P]
            return lambda ap: ap[:, 0:SEQ].rearrange("p (r c) -> p r c", c=GRID_W)[:, :, n * QC:(n + 1) * QC]

        def flow(l, kind):
            return [(pp, x) for pp in range(1 + kind) for x in units(l, kind)]

        def bodies(eng, kind, body):
            if kind == SWA:
                with eng.Fori(0, 2) as g:
                    body(g * 2, g, False)
            else:
                with eng.Fori(0, PAIRS - 1) as p:
                    body(p, None, True)
                body(PAIRS - 1, None, False)

        def rounds(eng, l, body, steps=None, per=0):
            n = HEADS * live_tiles(l)
            body(0, 0, True, False)
            with (steps.loop((n - 2) // 2, 2 * per) if steps else eng.Fori(0, (n - 2) // 2)) as i:
                body(i * 2 + 1, 1, False, False)
                body(i * 2 + 2, 0, False, False)
            body(n - 1, 1, False, True)

        block = ctx.enter_context(nc.Block())

        @block.sync
        def _(sp):
            for signal in (a_t, a_pt, a_o, a_oc, a_n):
                sp.sem_inc(signal, 2)
            for signal in (a_s, a_nm, a_p):
                sp.sem_inc(signal, 2)
            for signal in (a_z, a_zc, *s_mst):
                sp.sem_inc(signal, 1)
            sp.sem_inc(s_mod, AR)
            sp.dma_start(csil[:], t["cc"]).then_inc(s_cc, 16)
            for r in range(AR):
                sp.dma_start(ada[r], t["ada"][r]).then_inc(s_ada[r], 16)
                sp.dma_start(mrow[0:2, r, :], t["mrow"][r]).then_inc(s_ada[r], 16)
            for dst, name in ((ident, "ident"), (rope_cos, "rope_cos"), (rope_sin, "rope_sin"),
                              (na_mask, "na_mask"), (swa_mask, "swa_mask"), (iota, "iota")):
                sp.dma_start(dst[:], t[name]).then_inc(s_const, 16)
            sp.dma_start(X[:, 0:LT, :], t["x"][0].rearrange("(t p) d -> p t d", p=P)).then_inc(s_x, 16)
            sp.dma_start(X[:, LT:NT, :], t["ctx"][0].rearrange("(t p) d -> p t d", p=P)).then_inc(s_x, 16)
            with sp.Fori(0, DEPTH * MCH // AR - 1) as i:
                for r in range(AR):
                    sp.wait_ge(s_mod, AR * i + (AR + r + 1))
                    sp.dma_start(ada[r], t["ada"][AR * i + r + AR]).then_inc(s_ada[r], 16)
                    sp.dma_start(mrow[0:2, r, :], t["mrow"][AR * i + r + AR]).then_inc(s_ada[r], 16)

            def rows(l, which, parts, signal):
                for v in range(2):
                    for part in parts:
                        dst = gt[:, v] if part == 2 else modb[:, 2 * v + part]
                        for a in range(2):
                            row = t["mods_d"][l * MCH + 2 * (3 * which + part) + a, v:v + 1, :]
                            sp.dma_start(dst[:, a * 512:(a + 1) * 512], row.to_broadcast([P, 512])).then_inc(signal, 16)

            def shifts_scales(i):
                rows(i // 2, i % 2, (0, 1), n_in[i])

            def gate_rows(i):
                rows(i // 2, i % 2, (2,), s_gt)

            for r in range(AR):
                sp.wait_ge(s_mst[r], 1 + 16)
            shifts_scales(0)
            for r in range(AR):
                sp.wait_ge(s_mst[r], 1 + 16 * DEPTH * MCH // AR)
            for l in range(DEPTH):
                if l:
                    sp.wait_ge(f_acc, 2 + it_base[l])
                sp.dma_start(sinks[:], t["sink"][l:l + 1, :].to_broadcast([P, 8])).then_inc(s_sink[l], 16)
                o = 0
                for c, n in enumerate((512, 256, 512)):
                    sp.dma_start(w_tok[:, o:o + KB * n], t["w_tok"][l, :, o:o + KB * n]).then_inc(s_wt[l][c], 16)
                    o += KB * n
                sp.dma_start(wqk_first, t["wqk"][l * PAIRS]).then_inc(s_wqk, 16)
                gate_rows(2 * l)
                for i in range(NT):
                    sp.wait_ge(s_vst, l * NT + i + 1)
                    sp.dma_start(t["vn_d"][l, i * P:(i + 1) * P, :], vn_st[:, i % 2, :]).then_inc(s_vout[i % 2], 16)
                for r in range(2):
                    sp.wait_ge(s_vout[r], 16 * (l + 1) * NT // 2)
                grid = t["vn_d"][l, 0:SEQ, :].rearrange("(r c) d -> r c d", c=GRID_W)
                for n in range(NCB):
                    for half in range(2):
                        for r in range(4):
                            sp.dma_start(VN[r * KC:(r + 1) * KC, 2 * n + half, :],
                                         grid[4 * half + r, key_start(n):key_start(n) + KC, :]).then_inc(s_vn[l], 16)
                for i in range(CT):
                    sp.dma_start(VN[:, 8 + i, :], t["vn_d"][l, SEQ + i * P:SEQ + (i + 1) * P, :]).then_inc(s_vn[l], 16)
                sp.wait_ge(n_t, c_base[2 * l + 1])
                sp.dma_start(rpbT, t["rpb"][l]).then_inc(s_rpb[l], 16)
                sp.wait_ge(s_tz[0], (l + 1) * NT)
                sp.wait_ge(s_tz[1], (l + 1) * NT)
                sp.wait_ge(s_tz[2], q_base[l + 1])
                if ZN[l] == 4:
                    sp.dma_start(wqk[:, 0], t["wqk"][l * PAIRS, :, 0]).then_inc(s_wqk, 16)
                with sp.Fori(0, PAIRS - 1) as p:
                    sp.wait_ge(a_z, z_base(l) + ZN[l] + p * ZN[l])
                    sp.dma_start(wqk, t["wqk"][p + (l * PAIRS + 1)]).then_inc(s_wqk, 16)
                shifts_scales(2 * l + 1)
                sp.wait_ge(a_oc, unit_base(l, SWA))
                sp.dma_start(wpool, t["pool_w"][l]).then_inc(p_in, 16)
                sp.dma_start(pscale, t["pool_scale"][l]).then_inc(p_in, 16)
                for g in range(PAIRS):
                    if g >= 2:
                        sp.wait_ge(p_z, l * PAIRS + g - 1)
                    sp.dma_start(wa[:, g % 2], t["wa"][l, g]).then_inc(p_w[g % 2], 16)
                    if g:
                        sp.wait_ge(p_pool, l * PAIRS + g)
                    else:
                        sp.dma_start(wgb[0], t["wgb"][l * KB]).then_inc(m_w[0], 16)
                    sp.dma_start(inv_n, t["inv_n"][g:g + 1, :].to_broadcast([P, TOK])).then_inc(p_inv, 16)
                sp.wait_ge(p_z, (l + 1) * PAIRS)
                sp.dma_start(wgb[1], t["wgb"][l * KB + 1]).then_inc(m_w[1], 16)
                sp.wait_ge(p_ya, py_base[l + 1])
                for i in range(2):
                    sp.dma_start(wout_l[i], t["w_out"][l, 0, :, i * DB:(i + 1) * DB, :]).then_inc(s_wo[0], 16)
                with sp.Fori(0, KB // 2 - 1) as i:
                    for r in range(2):
                        sp.wait_ge(m_y, 3 * KB * l + 6 * i + 3 * r + 3)
                        sp.dma_start(wgb[r], t["wgb"][2 * i + (l * KB + r + 2)]).then_inc(m_w[r], 16)
                sp.wait_ge(m_y, 3 * KB * (l + 1))
                for i in range(2):
                    sp.dma_start(wout_r[i], t["w_out"][l, 1, :, i * DB:(i + 1) * DB, :]).then_inc(s_wo[1], 16)
                for r in range(2):
                    sp.dma_start(wqs[:, r], t["wqs"][l * 2 * HEADS + r]).then_inc(q_w[r], 16)
                sp.wait_ge(g_x, gx_base[l + 1])
                gate_rows(2 * l + 1)
                with sp.Fori(0, HEADS - 1) as i:
                    for r in range(2):
                        sp.wait_ge(q_s, 2 * HEADS * l + 2 * i + (r + 1))
                        sp.dma_start(wqs[:, r], t["wqs"][2 * i + (l * 2 * HEADS + r + 2)]).then_inc(q_w[r], 16)
                if l < DEPTH - 1:
                    shifts_scales(2 * l + 2)
            sp.dma_start(modb[:, 0, :], t["final_g"].unsqueeze(0).to_broadcast([P, D])).then_inc(n_in[2 * DEPTH], 16)
            for k in range(LT):
                sp.wait_ge(n_h, n_base[2 * DEPTH] + k + 1)
                sp.dma_start(t["out"][0, k * P:(k + 1) * P, :], H[:, k, :]).then_inc(s_store, 16)
            sp.wait_ge(s_store, 16 * LT)

        @block.tensor
        def _(pe):
            pe.wait_ge(s_silu, 1)
            with pe.Fori(0, DEPTH * MCH // AR) as i:
                for r in range(AR):
                    pe.wait_ge(s_ada[r], 32 * i + 32)
                    pe.wait_ge(s_mod, AR * i + (r + 1))
                    for k in range(KB):
                        mm = pe.matmul(PS[0:2, r, :], csil[:, k, :], ada[r][:, k, :], start=k == 0, stop=k == KB - 1)
                    mm.then_inc(s_mz, 1)

            pe.wait_ge(s_const, 16 * 6)

            def norm(i, tiles):
                for k in range(tiles):
                    pe.wait_ge(n_h, n_base[i] + k + 1)
                    for half in range(2):
                        x = 2 * k + half
                        if x >= 4:
                            pe.wait_ge(n_c, c_base[i] + x - 3)
                        for b in range(4):
                            mm = pe.transpose(PS[:, x % 4, b * P:(b + 1) * P],
                                              H[:, k, (4 * half + b) * P:(4 * half + b + 1) * P], ident[:])
                        mm.then_inc(n_t, 1)

            def tokens(l):
                nt = live_tiles(l)
                pe.wait_ge(n_c, c_base[2 * l + 1])

                def turn(k):
                    pe.wait_ge(s_kd, l * NT + k + 1)
                    if k:
                        pe.wait_ge(s_bc, bt_base[l] + k + min(k, nt))
                    for g in range(2):
                        mm = pe.transpose(PS[:, 6, g * P:(g + 1) * P], kdup[:, k % 2, g * P:(g + 1) * P], ident[:])
                    mm.then_inc(s_bt, 1)
                    if k < nt:
                        pe.wait_ge(s_qd, q_base[l] + k + 1)
                        for b in range(PAIRS):
                            mm = pe.transpose(PS[:, 7, b * P:(b + 1) * P], q_rot[:, k % 2, b * P:(b + 1) * P], ident[:])
                        mm.then_inc(s_bt, 1)

                for k in range(NT):
                    o = 0
                    for c, n in enumerate((512, 256, 512)):
                        w = w_tok[:, o:o + KB * n].rearrange("p (k n) -> p k n", n=n)
                        o += KB * n
                        if c == 2 and k >= nt:
                            continue
                        if k == 0:
                            pe.wait_ge(s_wt[l][c], 16)
                        if k >= 2:
                            if c == 0:
                                pe.wait_ge(s_vst, l * NT + k - 1)
                            elif c == 1:
                                pe.wait_ge(s_kd, l * NT + k - 1)
                            else:
                                pe.wait_ge(s_qd, q_base[l] + k - 1)
                        for kb in range(KB):
                            mm = pe.matmul(PS[:, 3 * (k % 2) + c, 0:n], hT[:, kb, k * P:(k + 1) * P], w[:, kb, :],
                                           start=kb == 0, stop=kb == KB - 1)
                        mm.then_inc(s_tz[c], 1)
                    if k:
                        turn(k - 1)
                turn(NT - 1)
                pe.wait_ge(s_vst, (l + 1) * NT)
                pe.wait_ge(s_bc, bt_base[l + 1])

            def attention(l, kind):
                todo = flow(l, kind)
                U = len(todo)

                def z(w, p, x, bank):
                    side, (t0, n) = (0, 1, 1, 0)[x], ((0, SEQ), (SEQ, CTX))[x // 2]
                    for k in range(KB):
                        mm = pe.matmul(PS[:, bank, 0:n], w[:, side, k, :], hT[:, k, t0:t0 + n],
                                       start=k == 0, stop=k == KB - 1)
                    mm.then_inc(a_z, 1)

                def body(p, g, more):
                    if kind == NA:
                        pe.wait_ge(a_zc, p * ZN[l] + (z_base(l) + 3))
                    else:
                        pe.wait_ge(a_sk, g * 3 + 3 * (2 * l + 1))
                    ub = p * UN[l] + unit_base(l, kind)
                    for u in range(U + 3):
                        if u < U:
                            pp, (what, hh, n, s0) = todo[u]
                            ks, qs = k_st[hh * HD:(hh + 1) * HD], (q_st, q_2nd)[pp][hh * HD:(hh + 1) * HD]
                            at = 1024 * (u % 2)
                            lhs = qs[:, (SEQ if what == "ctx" else 0) + n * P:(SEQ if what == "ctx" else 0) + (n + 1) * P]
                            if u >= 2:
                                pe.wait_ge(a_p, ub + (u - 1))
                            if what == "lat":
                                if kind == NA:
                                    rhs = ks[:, 0:SEQ].rearrange("p (r c) -> p r c", c=GRID_W)[
                                        :, :, key_start(n):key_start(n) + KC]
                                else:
                                    rhs = ks[:, max(n - 1, 0) * P:min(n + 2, LT) * P]
                                pe.matmul(PSF[:, at + s0:at + 512], lhs, rhs, start=True, stop=True)
                            pe.matmul(PSF[:, at + 512:at + 768], lhs, ks[:, SEQ:TOK], start=True, stop=True).then_inc(a_s, 1)
                        if u == 1 and kind == NA and ZN[l] == 4:
                            pe.wait_ge(s_wqk, p * 16 + 16 * ((PAIRS + 1) * l + 2))
                            pe.wait_ge(a_oc, ub)
                            z(wqk, p, 3, 7)
                        w = u - 3
                        if 0 <= w < U:
                            if w == 1 and kind == NA and ZN[l] == 4:
                                pe.wait_ge(a_zc, p * ZN[l] + (z_base(l) + 4))
                            pp, (what, hh, n, s0) = todo[w]
                            blocks = (768 - s0) // P
                            pe.wait_ge(a_pt, ub + (w + 1))
                            pe.wait_ge(a_oc, ub + (w - 1))
                            if w == 0:
                                pe.wait_ge(a_v, (g if kind == SWA else p) + (6 * l + 4 * kind + 1))
                            for b in range(5 - blocks, 5):
                                if kind == NA:
                                    v = v_st[:, (8 + b - 3) if b >= 3 else 2 * n + (b - 1), :]
                                else:
                                    v = vw_st[:, LT + b - 3 if b >= 3 else max(n - 1, 0) + b - (5 - blocks), :]
                                mm = pe.matmul(PS[:, 6 + w % 2, 0:P], v, probT[:, w % 2, b * P:(b + 1) * P],
                                               start=b == 5 - blocks, stop=b == 4)
                            mm.then_inc(a_o, 1)
                        w = u - 2
                        if 0 <= w < U:
                            blocks = (768 - todo[w][1][3]) // P
                            pe.wait_ge(a_n, ub + (w + 1))
                            pe.wait_ge(a_pt, ub + w)
                            for b in range(5 - blocks, 5):
                                mm = pe.transpose(PSF[:, 2048 + b * P:2048 + (b + 1) * P],
                                                  prob[:, w % 2, b * P:(b + 1) * P], ident[:])
                            mm.then_inc(a_t, 1)
                        if more and u >= U:
                            if u == U:
                                pe.wait_ge(s_wqk, p * 16 + 16 * ((PAIRS + 1) * l + ZN[l] - 1))
                            z(wqk, p + 1, u - U, u - U)

                if kind == NA:
                    pe.wait_ge(s_wqk, 16 * ((PAIRS + 1) * l + 1))
                    for x in range(3):
                        z(wqk_first, 0, x, x)
                bodies(pe, kind, body)

            def pool(l):
                groups = token_groups(l)
                ng = len(groups)

                def mix(g):
                    pe.wait_ge(p_pool, l * PAIRS + g + 1)
                    if g == 0:
                        pe.wait_ge(p_in, 32 * (l + 1))
                    else:
                        pe.wait_ge(p_ya, py_base[l] + ng * g)
                    for i, (t0, n) in enumerate(groups):
                        pe.matmul(PS[:, 4 + i, 0:n], wpool[:, g, :], pooled[:, t0:t0 + n], start=True, stop=True).then_inc(p_y, 1)

                for g in range(PAIRS):
                    pe.wait_ge(p_w[g % 2], 16 * (2 * l + g // 2 + 1))
                    if g >= 2:
                        pe.wait_ge(p_c, l * PAIRS + g - 1)
                    for i, (t0, n) in enumerate(groups):
                        for k in range(KB):
                            mm = pe.matmul(PS[:, 2 * (g % 2) + i, 0:n], wa[:, g % 2, k, :], hT[:, k, t0:t0 + n],
                                           start=k == 0, stop=k == KB - 1)
                    mm.then_inc(p_z, 1)
                    if g:
                        mix(g - 1)
                mix(PAIRS - 1)
                pe.wait_ge(p_ya, py_base[l + 1])

            def merge(l):
                groups = token_groups(l)
                base = 3 * KB * l
                with pe.Fori(0, KB // 2) as i:
                    for r in range(2):
                        pe.wait_ge(m_w[r], 16 * i + 16 * (l * KB // 2 + 1))
                        for b in range(3):
                            e = 3 * r + b
                            pe.wait_ge(m_m, 6 * i + (base + e + 1))
                            for s, (t0, n) in enumerate(groups):
                                for k in range(KB):
                                    mm = pe.matmul(PS[:, 4 * (e % 2) + s, 0:n], wgb[r][:, b * KB + k, :], hT[:, k, t0:t0 + n],
                                                   start=k == 0, stop=k == KB - 1)
                            mm.then_inc(m_z, 1)
                            for s, (t0, n) in enumerate(groups):
                                for k in range(PAIRS):
                                    mm = pe.matmul(PS[:, 4 * (e % 2) + 2 + s, 0:n], wgb[r][:, 3 * KB + b * PAIRS + k, :],
                                                   oT[b][:, k, t0:t0 + n], start=k == 0, stop=k == PAIRS - 1)
                            mm.then_inc(m_y, 1)

            def out_projection(l):
                pe.wait_ge(m_m, 2 + 3 * KB * (l + 1))
                nt = live_tiles(l)
                for x in range(2 * nt):
                    half, k = x // nt, x % nt
                    if k == 0:
                        pe.wait_ge(s_wo[half], 32 * (l + 1))
                    if x >= 4:
                        pe.wait_ge(g_x, gx_base[l] + x - 3)
                    for kb in range(KB):
                        mm = pe.matmul(PS[:, x % 4, :], mT[:, kb, k * P:(k + 1) * P], (wout_l, wout_r)[half][kb // DB][:, kb % DB, :],
                                       start=kb == 0, stop=kb == KB - 1)
                    mm.then_inc(g_z, 1)

            def queries(l):
                groups, nt = token_groups(l), live_tiles(l)
                ng = len(groups)
                pe.wait_ge(n_c, c_base[2 * l + 2])
                pe.wait_ge(g_x, gx_base[l + 1])
                with pe.Fori(0, HEADS) as i:
                    for r in range(2):
                        pe.wait_ge(q_w[r], 16 * i + 16 * (l * HEADS + 1))
                        for s, (t0, n) in enumerate(groups):
                            for k in range(KB):
                                mm = pe.matmul(PS[:, 4 * r + s, 0:n], wqs[:, r, k, :], hT[:, k, t0:t0 + n],
                                               start=k == 0, stop=k == KB - 1)
                            mm.then_inc(q_z, 1)
                        pe.wait_ge(q_sc, 2 * i + (2 * HEADS * l + r + 1))
                        for k in range(nt):
                            if k % LT == 0:
                                pe.wait_ge(q_c, 2 * ng * i + (qz_base[l] + r * ng + k // LT + 1))
                            mm = pe.matmul(PSF[:, 2048 * r + 1024 + k * P:2048 * r + 1024 + (k + 1) * P],
                                           qb[:, r, k * P:(k + 1) * P], wqs[:, r, KB, :], start=True, stop=True)
                        mm.then_inc(q_s, 1)

            def experts(l):
                pe.wait_ge(q_sc, 2 + 2 * HEADS * (l + 1))
                with pe.Fori(0, live_tiles(l)) as k:
                    with pe.Fori(0, HEADS // 2) as hp:
                        for e in range(2):
                            it = k * HEADS + hp * 2 + (it_base[l] + e)
                            pe.wait_ge(f_acc, it + 1)
                            for s in range(TOPK):
                                pe.wait_ge(f_dg, it * TOPK + (s + 1))
                                pe.wait_ge(g_v[s % RING], it * 32 + 16 * (s // RING + 1))
                                for half in range(2):
                                    mm = pe.matmul(PS[:, 2 * e + half, :], diag[:, s % 4, :],
                                                   V[:, s % RING, half * 512:(half + 1) * 512],
                                                   start=s == 0, stop=s == TOPK - 1)
                                mm.then_inc(v_free, 1)

            for l in range(DEPTH):
                norm(2 * l, NT)
                tokens(l)
                attention(l, NA)
                attention(l, SWA)
                pool(l)
                merge(l)
                out_projection(l)
                norm(2 * l + 1, live_tiles(l))
                queries(l)
                experts(l)

        @block.scalar
        def _(act):
            act.wait_ge(s_cc, 16)
            act.activation(att[:, 0:4, :].rearrange("p a b -> p (a b)"), csil[:].rearrange("p k v -> p (k v)"),
                           ACT.Sigmoid).then_inc(s_sg, 1)
            with act.Fori(0, DEPTH * MCH // AR) as i:
                for r in range(AR):
                    act.wait_ge(s_mod, AR * i + (AR + r + 1))
                    act.dma_start(t["mods_d"][AR * i + r], mout[0:2, r, :]).then_inc(s_mst[r], 16)

            act.wait_ge(s_const, 16 * 6)

            def norm(i, tiles):
                act.wait_ge(n_ss, i + 1)
                act.activation(ss[:, 2, :], ss[:, 1, :], ACT.Sqrt).then_inc(n_sq, 1)
                for x in range(2 * tiles):
                    k, half = x // 2, x % 2
                    act.wait_ge(n_t, c_base[i] + x + 1)
                    act.activation(hT[:, 4 * half:4 * half + 4, k * P:(k + 1) * P],
                                   PS[:, x % 4, :].rearrange("p (b n) -> p b n", n=P), ACT.Copy).then_inc(n_c, 1)

            def tokens(l):
                nt = live_tiles(l)

                def turn(k):
                    cols = slice(k * P, (k + 1) * P)
                    act.wait_ge(s_bt, bt_base[l] + k + min(k, nt) + 1)
                    act.activation(kwT[:, :, cols], PS[:, 6, 0:2 * P].rearrange("p (g n) -> p g n", n=P), ACT.Copy).then_inc(s_bc, 1)
                    if k < nt:
                        act.wait_ge(s_bt, bt_base[l] + k + min(k, nt) + 2)
                        act.activation(qwT[:, :, cols], PS[:, 7, :].rearrange("p (g n) -> p g n", n=P), ACT.Copy).then_inc(s_bc, 1)

                for k in range(NT):
                    act.wait_ge(s_tz[0], l * NT + k + 1)
                    done = l * NT // 2 + k // 2
                    if k >= 2:
                        act.wait_ge(s_vout[k % 2], 16 * done)
                    act.activation(vn_st[:, k % 2, :], PS[:, 3 * (k % 2), :], ACT.Copy).then_inc(s_vst, 1)
                    if k:
                        turn(k - 1)
                turn(NT - 1)

            def attention(l, kind):
                todo = flow(l, kind)
                U = len(todo)
                nq = SEQ if ZN[l] == 3 else TOK
                if kind == NA:
                    act.wait_ge(s_tz[2], q_base[l + 1])
                    act.wait_ge(s_bt, bt_base[l + 1])

                def copy(p, x, bank):
                    dst, (t0, n) = (q_st, k_st, k_st, q_st)[x], ((0, SEQ), (SEQ, CTX))[x // 2]
                    act.wait_ge(a_z, p * ZN[l] + (z_base(l) + x + 1))
                    out, src = dst[:, t0:t0 + n], PS[:, bank, 0:n]
                    if x == 0:
                        out = out.rearrange("p (n r c) -> p n r c", r=ROWS, c=QC)
                        src = src.rearrange("p (r n c) -> p n r c", n=NCB, c=QC)
                    act.activation(out, src, ACT.Copy).then_inc(a_zc, 1)

                def body(p, g, more):
                    if kind == SWA:
                        act.activation(k_st, kwT[:, g, :], ACT.Copy).then_inc(a_sk, 1)
                        for pp, q in enumerate((q_st, q_2nd)):
                            act.activation(q[:, 0:nq], qwT[:, p + pp, 0:nq], ACT.Copy).then_inc(a_sk, 1)
                    ub = p * UN[l] + unit_base(l, kind)
                    for u in range(U + 3 + more):
                        w = u - 3
                        if 0 <= w < U:
                            pp, (what, hh, n, s0) = todo[w]
                            half = slice(hh * HD, (hh + 1) * HD)
                            act.wait_ge(a_o, ub + (w + 1))
                            src = PS[half, 6 + w % 2, 0:P]
                            dst = q_tokens(kind, what, n)(oT[1 + kind][half, p + pp, :])
                            if what == "lat" and kind == NA:
                                src = src.rearrange("p (r c) -> p r c", c=QC)
                            act.activation(dst, src, ACT.Copy).then_inc(a_oc, 1)
                        w = u - 2
                        if 0 <= w < U:
                            lo = todo[w][1][3] - P
                            act.wait_ge(a_t, ub + (w + 1))
                            if w >= 2:
                                act.wait_ge(a_o, ub + (w - 1))
                            act.activation(probT[:, w % 2, lo:640], PSF[:, 2048 + lo:2048 + 640], ACT.Copy).then_inc(a_pt, 1)
                        if u < U:
                            pp, (what, hh, n, s0) = todo[u]
                            c = att[:, u % 8, :]
                            at = 1024 * (u % 2)
                            act.wait_ge(a_nm, ub + (u + 1))
                            if u >= 2:
                                act.wait_ge(a_t, ub + (u - 1))
                            ins = act.activation(prob[:, u % 2, s0 - P:640], PSF[:, at + s0:at + 768], ACT.Exp,
                                                 bias=c[:, 1:2], scale=SCALE, accum_out=c[:, 2:3])
                            if kind == SWA:
                                ins = act.activation(c[:, 3:4], sink_st[:, 2 * pp + hh:2 * pp + hh + 1], ACT.Exp, bias=c[:, 1:2])
                            ins.then_inc(a_p, 1)
                        if u == 1 and kind == NA and ZN[l] == 4:
                            copy(p, 3, 7)
                        if u == 1:
                            act.wait_ge(a_o, ub)
                            if kind == NA:
                                act.activation(v_st, VN[:, :, bass.ds(p * P, P)], ACT.Copy).then_inc(a_v, 1)
                            else:
                                act.activation(vw_st[:, :, 0:HD], Vw[:, :, bass.ds(g * HD, HD)], ACT.Copy)
                                act.activation(vw_st[:, :, HD:P], Vw[:, :, bass.ds(g * HD, HD)], ACT.Copy).then_inc(a_v, 1)
                        if more and u > U:
                            copy(p + 1, u - U - 1, u - U - 1)

                if kind == NA:
                    for x in range(3):
                        copy(0, x, x)
                    act.wait_ge(s_vn[l], 16 * (8 * 4 + CT))
                bodies(act, kind, body)

            def pool(l):
                groups = token_groups(l)
                ng = len(groups)

                def mix(g):
                    for i, (t0, n) in enumerate(groups):
                        act.wait_ge(p_y, py_base[l] + ng * g + i + 1)
                        act.activation(oT[0][:, g, t0:t0 + n], PS[:, 4 + i, 0:n], ACT.Copy, scale=pscale[:, g:g + 1]).then_inc(p_ya, 1)

                act.wait_ge(p_pad, l + 1)
                act.wait_ge(p_in, 32 * (l + 1))
                for g in range(PAIRS):
                    act.wait_ge(p_z, l * PAIRS + g + 1)
                    if g:
                        act.wait_ge(p_pool, l * PAIRS + g)
                    for i, (t0, n) in enumerate(groups):
                        o = PADL if i == 0 else 3 * PADL + SEQ
                        ins = act.activation(a_pad[:, o:o + n], PS[:, 2 * (g % 2) + i, 0:n], ACT.Copy)
                    ins.then_inc(p_c, 1)
                    if g:
                        mix(g - 1)
                mix(PAIRS - 1)

            def merge(l):
                n = live_tiles(l) * P
                base = 3 * KB * l
                with act.Fori(0, KB // 2) as i:
                    for e in range(6):
                        act.wait_ge(m_z, 6 * i + (base + e + 1))
                        act.wait_ge(m_m, 6 * i + (base + e + 1))
                        act.activation(sig[:, e % 2, 0:n], PSF[:, 2048 * (e % 2):2048 * (e % 2) + n], ACT.Sigmoid).then_inc(m_sig, 1)

            def queries(l):
                groups = token_groups(l)
                ng = len(groups)
                with act.Fori(0, HEADS) as i:
                    for r in range(2):
                        for s, (t0, n) in enumerate(groups):
                            act.wait_ge(q_z, 2 * ng * i + (qz_base[l] + r * ng + s + 1))
                            if s == 0:
                                act.wait_ge(q_sc, 2 * i + (2 * HEADS * l + r + 1))
                            act.activation(qb[:, r, t0:t0 + n], PS[:, 4 * r + s, 0:n], ACT.Copy).then_inc(q_c, 1)

            def experts(l):
                act.wait_ge(q_s, 2 * HEADS * (l + 1))

                def exps(n, e):
                    act.wait_ge(f_nm, n + (it_base[l] + 1))
                    act.activation(top_ex[:, e, :], best[:], ACT.Exp, bias=red[:, 0:1],
                                   accum_out=red[:, 1 + 2 * e:2 + 2 * e]).then_inc(f_ex, 1)

                def diagonals(n, e, slots):
                    act.wait_ge(f_w, n + (it_base[l] + 1))
                    for s in slots:
                        act.wait_ge(v_free, n * TOPK + (it_base[l] * TOPK + RING + s - 3))
                        act.activation(diag[:, s % 4, :], ident[:], ACT.Copy, scale=wgt[:, e, s:s + 1]).then_inc(f_dg, 1)

                def body(n, e, first, last):
                    if not first:
                        diagonals(n - 1, 1 - e, range(0, TOPK // 2))
                    if not last:
                        exps(n + 1, 1 - e)
                    if not first:
                        diagonals(n - 1, 1 - e, range(TOPK // 2, TOPK))
                    act.wait_ge(u_free, n * TOPK + (it_base[l] * TOPK + RING + TOPK))
                    act.activation(act_out[:, e, :], act_in[:, e, :], ACT.Gelu).then_inc(f_gel, 1)

                exps(0, 0)
                rounds(act, l, body)
                diagonals(HEADS * live_tiles(l) - 1, 1, range(TOPK))

            for l in range(DEPTH):
                norm(2 * l, NT)
                tokens(l)
                attention(l, NA)
                attention(l, SWA)
                pool(l)
                merge(l)
                norm(2 * l + 1, live_tiles(l))
                queries(l)
                experts(l)
            act.wait_ge(n_ss, norms)
            act.activation(ss[:, 2, :], ss[:, 1, :], ACT.Sqrt).then_inc(n_sq, 1)

        @block.vector
        def _(dve):
            step = Steps(dve, s_dve)

            def square(k):
                step.done(dve.tensor_tensor_reduce(H[:, k, :], X[:, k, :], X[:, k, :], 1.0, 0.0, ALU.mult, ALU.add, ss[:, 0, k:k + 1]))

            dve.memset(red[:, 0:1], 0.0).then_inc(u_free, RING)
            dve.memset(red[:, 1:2], 0.0).then_inc(v_free, RING)
            dve.memset(red[:, 2:3], 0.0).then_inc(f_acc, 2)
            dve.memset(red[:, 3:4], 0.0).then_inc(m_m, 2)
            dve.memset(ss[:], 1.0).then_inc(q_sc, 2)
            dve.wait_ge(s_sg, 1)
            dve.tensor_tensor(csil[:], csil[:], att[:, 0:4, :].rearrange("p a (b v) -> p (a b) v", v=2), ALU.mult).then_inc(s_silu, 1)

            def modulation(first, count):
                with step.loop(count, 2 * AR) as i:
                    for r in range(AR):
                        dve.wait_ge(s_mz, AR * i + (AR * first + r + 1))
                        dve.wait_ge(s_mst[r], 16 * i + (16 * first + 1))
                        row = mout[0:2, r, :]
                        step.done(dve.tensor_tensor(row, PS[0:2, r, :], mrow[0:2, r, 0:512], ALU.add))
                        step.done(dve.tensor_tensor(row, row, mrow[0:2, r, 512:1024], ALU.add))
                        dve.tensor_tensor(row, row, mrow[0:2, r, 1024:1536], ALU.mult).then_inc(s_mod, 1)

            chunks = DEPTH * MCH // AR
            modulation(0, chunks // 2)
            dve.wait_ge(s_const, 16 * 6)
            dve.wait_ge(s_x, 32)
            dve.wait_ge(q_sc, 2)
            for k in range(NT):
                square(k)
            modulation(chunks // 2, chunks - chunks // 2)

            def rstd(i):
                dve.tensor_scalar(ss[:, 1, :], ss[:, 0, :], 1.0 / D, EPS, ALU.mult, ALU.add).then_inc(n_ss, 1)
                dve.wait_ge(n_sq, i + 1)
                step.done(dve.reciprocal(ss[:, 0, :], ss[:, 2, :]))

            def norm(l, which, tiles):
                i = 2 * l + which
                rstd(i)
                dve.wait_ge(n_in[i], 16 * 8)
                for k in range(tiles):
                    v = 0 if k < LT else 1
                    step.done(dve.scalar_tensor_tensor(H[:, k, :], X[:, k, :], ss[:, 0, k:k + 1], modb[:, 2 * v + 1, :], ALU.mult, ALU.mult))
                    dve.tensor_tensor(H[:, k, :], H[:, k, :], modb[:, 2 * v, :], ALU.add).then_inc(n_h, 1)

            def rotate(dst, src, nh, k):
                heads = lambda ap: ap.rearrange("p (h d) -> p h d", d=HD)
                wide = lambda ap: ap.rearrange("p (h a s f) -> p h a s f", a=2, s=2, f=16)
                step.done(dve.tensor_tensor(heads(dst), heads(src), rope_cos[:, k, :].unsqueeze(1).to_broadcast([P, nh, HD]), ALU.mult))
                tmp = r_tmp[:, 0:nh * HD]
                sin = rope_sin[:, k, :].rearrange("p (a s f) -> p a s f", s=2, f=16)
                for s in range(2):
                    step.done(dve.tensor_tensor(wide(tmp)[:, :, :, s, :], wide(src)[:, :, :, 1 - s, :],
                                                sin[:, :, s, :].unsqueeze(1).to_broadcast([P, nh, 2, 16]), ALU.mult))
                return dve.tensor_tensor(dst, dst, tmp, ALU.add)

            def tokens(l):
                nt = live_tiles(l)
                for k in range(NT):
                    if k >= 2:
                        dve.wait_ge(s_bt, bt_base[l] + (k - 1) + min(k - 1, nt))
                    kd = kdup[:, k % 2, :].rearrange("p (g u d) -> p g u d", u=2, d=HD)
                    dve.wait_ge(s_tz[1], l * NT + k + 1)
                    if k:
                        dve.wait_ge(s_kd, l * NT + k)
                    dve.tensor_copy(Vw[:, k, :], PS[:, 3 * (k % 2) + 1, P:2 * P])
                    src = PS[:, 3 * (k % 2) + 1, 0:P]
                    if k < LT:
                        step.done(rotate(k_rot, src, 2, k))
                    else:
                        step.done(dve.tensor_copy(k_rot, src))
                    for u in range(2):
                        ins = dve.tensor_copy(kd[:, :, u, :], k_rot.rearrange("p (g d) -> p g d", d=HD))
                    ins.then_inc(s_kd, 1)
                    if k < nt:
                        dve.wait_ge(s_tz[2], q_base[l] + k + 1)
                        src = PS[:, 3 * (k % 2) + 2, :]
                        if k < LT:
                            ins = rotate(q_rot[:, k % 2, :], src, HEADS, k)
                        else:
                            ins = dve.tensor_copy(q_rot[:, k % 2, :], src)
                        ins.then_inc(s_qd, 1)

            def softmax_bias(kind, todo, u, head):
                _, (what, hh, n, s0) = todo[u]
                at = 1024 * (u % 2)
                if what == "ctx":
                    return 0
                if kind == NA:
                    s = PSF[:, at + s0:at + 512].rearrange("p (r c) -> p r c", c=KC)
                    w0 = key_start(n) - n * QC + 16
                    step.done(dve.scalar_tensor_tensor(s, rpbT[:, head, :, w0:w0 + KC], 1.0 / SCALE, s, ALU.mult, ALU.add))
                    step.done(dve.tensor_tensor(s, s, na_mask[:, n, :].unsqueeze(1).to_broadcast([P, ROWS, KC]), ALU.add))
                    return 2
                steps = 0
                for side, there, lo in ((0, n > 0, s0), (1, n < LT - 1, 512 - P)):
                    if there:
                        s = PSF[:, at + lo:at + lo + P]
                        step.done(dve.tensor_tensor(s, s, swa_mask[:, side, :], ALU.add))
                        steps += 1
                return steps

            def attention(l, kind):
                todo = flow(l, kind)
                U = len(todo)
                lat = 2 * NCB
                per = 2 * lat + 2 * U if kind == NA else 2 * 4 * (NCB - 1) + 4 * U + 1
                if kind == NA:
                    dve.wait_ge(s_rpb[l], 16)
                else:
                    dve.wait_ge(s_sink[l], 16)
                with step.loop(2 if kind == SWA else PAIRS, per) as g:
                    p = g * 2 if kind == SWA else g
                    ub = p * UN[l] + unit_base(l, kind)
                    if kind == SWA:
                        step.done(dve.tensor_copy(sink_st[:], sinks[:, bass.ds(p * 2, 4)]))
                    for u in range(U + 1):
                        if u < U:
                            pp, (what, hh, n, s0) = todo[u]
                            at = 1024 * (u % 2)
                            c = att[:, u % 8, :]
                            dve.wait_ge(a_s, ub + (u + 1))
                            softmax_bias(kind, todo, u, p * 2 + hh)
                            step.done(dve.tensor_reduce(c[:, 0:1], PSF[:, at + s0:at + 768], AX.X, ALU.max))
                            if kind == SWA:
                                step.done(dve.tensor_scalar(c[:, 0:1], c[:, 0:1], SCALE, sink_st[:, 2 * pp + hh:2 * pp + hh + 1], ALU.mult, ALU.max))
                                dve.tensor_scalar(c[:, 1:2], c[:, 0:1], -1.0, None, ALU.mult).then_inc(a_nm, 1)
                            else:
                                dve.tensor_scalar(c[:, 1:2], c[:, 0:1], -SCALE, None, ALU.mult).then_inc(a_nm, 1)
                        w = u - 1
                        if 0 <= w < U:
                            c = att[:, w % 8, :]
                            dve.wait_ge(a_p, ub + (w + 1))
                            if kind == SWA:
                                step.done(dve.tensor_tensor(c[:, 2:3], c[:, 2:3], c[:, 3:4], ALU.add))
                            step.done(dve.reciprocal(c[:, 0:1], c[:, 2:3]))
                            part = prob[:, w % 2, todo[w][1][3] - P:640]
                            dve.tensor_scalar(part, part, c[:, 0:1], None, ALU.mult).then_inc(a_n, 1)

            def pool(l):
                groups = token_groups(l)
                dve.wait_ge(a_o, unit_base(l, SWA) + PAIRS * UN[l])
                dve.memset(a_pad, 0.0).then_inc(p_pad, 1)
                for g, w in enumerate(POOLS):
                    dve.wait_ge(p_c, l * PAIRS + g + 1)
                    dve.wait_ge(p_inv, 16 * (l * PAIRS + g + 1))
                    if g:
                        dve.wait_ge(p_y, py_base[l] + len(groups) * g)
                    src, length, have = a_pad, PADW, 1
                    while have < w:
                        dst = win[:, have.bit_length() % 2, :]
                        length -= have
                        step.done(dve.tensor_tensor(dst[:, 0:length], src[:, 0:length], src[:, have:have + length], ALU.add))
                        src, have = dst, 2 * have
                    for i, (t0, n) in enumerate(groups):
                        o = PADL if i == 0 else 3 * PADL + SEQ
                        step.done(dve.tensor_tensor(pooled[:, t0:t0 + n], src[:, o - w // 2:o - w // 2 + n], inv_n[:, t0:t0 + n], ALU.mult))
                        ins = dve.tensor_tensor(pooled[:, t0:t0 + n], pooled[:, t0:t0 + n], a_pad[:, o:o + n], ALU.subtract)
                    ins.then_inc(p_pool, 1)

            def merge(l):
                n = live_tiles(l) * P
                base = 3 * KB * l
                with step.loop(KB // 2, 4) as i:
                    for r in range(2):
                        for b in range(3):
                            e = 3 * r + b
                            gate_b, y = sig[:, e % 2, 0:n], PSF[:, 2048 * (e % 2) + 1024:2048 * (e % 2) + 1024 + n]
                            row = mT[:, 2 * i + r, 0:n]
                            dve.wait_ge(m_sig, 6 * i + (base + e + 1))
                            dve.wait_ge(m_y, 6 * i + (base + e + 1))
                            if b == 0:
                                dve.tensor_tensor(row, gate_b, y, ALU.mult).then_inc(m_m, 1)
                            else:
                                dve.wait_ge(m_m, 6 * i + (base + e + 2))
                                step.done(dve.tensor_tensor(mtmp[:, 0:n], gate_b, y, ALU.mult))
                                dve.tensor_tensor(row, row, mtmp[:, 0:n], ALU.add).then_inc(m_m, 1)

            def out_projection(l):
                nt = live_tiles(l)
                dve.wait_ge(s_gt, 64 * (2 * l + 1))
                for x in range(2 * nt):
                    half, k = x // nt, x % nt
                    cols = slice(half * 512, (half + 1) * 512)
                    dve.wait_ge(g_z, gx_base[l] + x + 1)
                    if x == 0:
                        dve.wait_ge(m_m, 2 + 3 * KB * (l + 1))
                    if x >= 2:
                        dve.wait_ge(g_x, gx_base[l] + x - 1)
                    step.done(dve.tensor_tensor(xtmp[:, x % 2, :], PS[:, x % 4, :], gt[:, 0 if k < LT else 1, cols], ALU.mult))
                    dve.tensor_tensor(X[:, k, cols], X[:, k, cols], xtmp[:, x % 2, :], ALU.add).then_inc(g_x, 1)
                    if half:
                        dve.wait_ge(g_x, gx_base[l] + x + 1)
                        square(k)
                dve.wait_ge(g_x, gx_base[l + 1])

            def queries(l):
                nt = live_tiles(l)
                table = S_all[:, 0:NT * 2 * HEADS * P].rearrange("p (k b n) -> p k b n", k=NT, n=P)
                with dve.Fori(0, HEADS) as i:
                    for r in range(2):
                        dve.wait_ge(q_s, 2 * i + (2 * HEADS * l + r + 1))
                        dve.tensor_copy(table[:, 0:nt, 2 * i + r, :],
                                        PSF[:, 2048 * r + 1024:2048 * r + 1024 + nt * P].rearrange("p (k n) -> p k n", n=P)).then_inc(q_sc, 1)
                dve.wait_ge(q_sc, 2 + 2 * HEADS * (l + 1))

            def top16(values, indices, rows, cut):
                step.done(dve.max(values[:, 0:8], rows), s_held)
                dve.max_index(indices[:, 0:8], values[:, 0:8], rows)
                step.done(dve.match_replace(cut, values[:, 0:8], rows, LOW), s_held)
                step.done(dve.max(values[:, 8:16], cut), s_held)
                return dve.max_index(indices[:, 8:16], values[:, 8:16], cut)

            def route(n, e, l):
                step.done(dve.tensor_copy(s_st.rearrange("p a n -> p (a n)"), S_all[:, bass.ds(n * (2 * P), 2 * P)]), s_held)
                for side in range(2):
                    ins = top16(v16[:, side, :], i16[:, side, :], s_st[:, side, :], s_cut[:, side, :])
                    step.done(ins, s_held)
                dve.tensor_scalar(code[:, 0:TOPK], i16[:, 0, :], float(NKEYS), None, ALU.mult)
                step.done(dve.tensor_copy(code[:, TOPK:2 * TOPK], i16[:, 1, :]))
                step.done(dve.tensor_tensor(cand, v16[:, 0, :].unsqueeze(2).to_broadcast([P, TOPK, TOPK]),
                                            v16[:, 1, :].unsqueeze(1).to_broadcast([P, TOPK, TOPK]), ALU.add), s_held)
                flat = cand.rearrange("p a b -> p (a b)")
                if not (isinstance(n, int) and n == 0):
                    dve.wait_ge(f_ex, n + it_base[l])
                    dve.sem_inc(s_held, 1)
                step.done(top16(best, best_j, flat, cand_cut.rearrange("p a b -> p (a b)")))
                dve.tensor_scalar(red[:, 0:1], best[:, 0:1], -1.0, None, ALU.mult).then_inc(f_nm, 1)
                step.done(dve.tensor_scalar(ab_u[:, :, 0], best_j[:], 4, None, ALU.logical_shift_right))
                step.done(dve.tensor_scalar(ab_u[:, :, 1], best_j[:], 15, None, ALU.bitwise_and))
                step.done(dve.tensor_copy(ab[:], ab_u[:]))
                oh = onehot.rearrange("p k (s j) -> p k s j", s=2)
                step.done(dve.tensor_tensor(oh, ab[:].unsqueeze(3).to_broadcast([P, TOPK, 2, TOPK]),
                                            iota[:].unsqueeze(1).unsqueeze(1).to_broadcast([P, TOPK, 2, TOPK]), ALU.is_equal))
                step.done(dve.tensor_tensor(onehot, onehot, code[:].unsqueeze(1).to_broadcast([P, TOPK, 2 * TOPK]), ALU.mult))
                step.done(dve.tensor_reduce(expert_f[:], onehot, AX.X, ALU.add))
                dve.tensor_copy(expert_u[:, e, :], expert_f[:]).then_inc(f_idx, 1)

            def experts(l):
                base = it_base[l]

                def products(n, e, slots):
                    for s in slots:
                        dve.wait_ge(g_u[s % RING], n * 32 + (base * 32 + 16 * (s // RING + 1)))
                        row = U[:, s % RING, :]
                        dve.tensor_tensor_reduce(row, row, h_st, 1.0, 0.0, ALU.mult, ALU.add,
                                                 act_in[:, e, s:s + 1]).then_inc(u_free, 1)

                def update(n, e):
                    tile = n // HEADS
                    v = 0 if l == DEPTH - 1 else tile // LT
                    row = X[:, tile, :]
                    dve.wait_ge(v_free, n * TOPK + (base * TOPK + RING + TOPK))
                    dve.tensor_tensor(x_upd, PSF[:, 1024 * e:1024 * (e + 1)], gt[:, v, :], ALU.mult).then_inc(f_acc, 1)
                    dve.wait_ge(f_acc, n + (base + 3))
                    step.done(dve.tensor_tensor(row, row, x_upd, ALU.add))

                def body(n, e, first, last):
                    step.done(dve.tensor_copy(h_st, H[:, n // HEADS, :]))
                    dve.tensor_copy(expert_v[:, e, :], expert_u[:, e, :]).then_inc(f_vidx, 1)
                    products(n, e, range(0, 4))
                    if not last:
                        route(n + 1, 1 - e, l)
                    products(n, e, range(4, TOPK))
                    dve.wait_ge(f_ex, n + (base + 1))
                    step.done(dve.reciprocal(red[:, 2:3], red[:, 1 + 2 * e:2 + 2 * e]))
                    step.done(dve.tensor_scalar(gate[:, e, :], top_ex[:, e, :], red[:, 2:3], None, ALU.mult))
                    dve.wait_ge(f_gel, n + (base + 1))
                    dve.tensor_tensor(wgt[:, e, :], gate[:, e, :], act_out[:, e, :], ALU.mult).then_inc(f_w, 1)
                    if not first:
                        update(n - 1, 1 - e)

                dve.wait_ge(s_gt, 64 * (2 * l + 2))
                first = step.n
                route(0, 0, l)
                rounds(dve, l, body, step, step.n - first + 4)
                tiles = live_tiles(l)
                for k in range(tiles - 1):
                    square(k)
                update(HEADS * tiles - 1, 1)
                square(tiles - 1)

            for l in range(DEPTH):
                norm(l, 0, NT)
                tokens(l)
                attention(l, NA)
                attention(l, SWA)
                pool(l)
                merge(l)
                out_projection(l)
                norm(l, 1, live_tiles(l))
                queries(l)
                experts(l)
            rstd(2 * DEPTH)
            dve.wait_ge(n_in[2 * DEPTH], 16)
            for k in range(LT):
                dve.scalar_tensor_tensor(H[:, k, :], X[:, k, :], ss[:, 0, k:k + 1], modb[:, 0, :], ALU.mult, ALU.mult).then_inc(n_h, 1)

        @block.gpsimd
        def _(pool):
            for l in range(DEPTH):
                base = it_base[l]
                pool.wait_ge(q_s, 2 * HEADS * (l + 1))

                def gather(ring, table, places, free, landed, n, s):
                    pool.wait_ge(free, n * TOPK + (base * TOPK + s + 1))
                    if not isinstance(n, int):
                        pool.sem_inc(s_held, 1)
                    pool.indirect_dma_start(ring[:, s % RING, :], None, table, bass.IndirectOffsetOnAxis(
                        ap=places[:, s:s + 1], axis=0)).then_inc(landed[s % RING], 16)

                def body(n, e, first, last):
                    pool.wait_ge(f_idx, n + (base + 1))
                    if not first:
                        pool.wait_ge(f_vidx, n + base)
                    for s in range(TOPK):
                        gather(U, t["peer_u"][l], expert_u[:, e, :], u_free, g_u, n, s)
                        if not first:
                            gather(V, t["peer_v"][l], expert_v[:, 1 - e, :], v_free, g_v, n - 1, s)

                rounds(pool, l, body)
                n = HEADS * live_tiles(l)
                pool.wait_ge(f_vidx, n + base)
                for s in range(TOPK):
                    gather(V, t["peer_v"][l], expert_v[:, 1, :], v_free, g_v, n - 1, s)


def constants(np):
    inv = 10000.0 ** (-np.arange(16, dtype=np.float32) / np.float32(16))
    tok = np.arange(SEQ)
    ang = np.stack([(tok // GRID_W).astype(np.float32), (tok % GRID_W).astype(np.float32)], 1)[:, :, None] * inv.astype(np.float32)
    cos, sin = np.cos(ang), np.sin(ang)
    tiles = lambda a: np.ascontiguousarray(a.reshape(LT, P, HD).transpose(1, 0, 2).astype(np.float32))
    q = np.arange(P) % QC
    mask = np.full((P, NCB, KC), MASKED, np.float32)
    for n in range(NCB):
        start = np.clip(n * QC + q - 8, 0, GRID_W - 16)[:, None]
        col = key_start(n) + np.arange(KC)[None, :]
        mask[:, n, :][(col >= start) & (col < start + 16)] = 0.0
    i, j = np.arange(P)[:, None], np.arange(P)[None, :]
    swa = np.stack([np.where(j >= i, 0.0, MASKED), np.where(j <= i, 0.0, MASKED)], 1).astype(np.float32)
    inv_n = np.zeros((PAIRS, TOK), np.float32)
    for g, w in enumerate(POOLS):
        for t0, n in ((0, SEQ), (SEQ, CTX)):
            x = np.arange(n)
            inv_n[g, t0:t0 + n] = 1.0 / (np.clip(x - w // 2 + w, 0, n) - np.clip(x - w // 2, 0, n))
    return {
        "ident": np.eye(P, dtype=np.float32),
        "rope_cos": tiles(np.stack([cos, cos], 2)), "rope_sin": tiles(np.stack([-sin, sin], 2)),
        "na_mask": mask, "swa_mask": swa, "inv_n": inv_n,
        "iota": np.tile(np.arange(TOPK, dtype=np.float32), (P, 1)),
    }


def layouts(np, i):
    c = np.ascontiguousarray
    blocks = lambda w: w.reshape(KB, P, -1).transpose(1, 0, 2)
    w_in = i["w_in"]
    VNc, KWc, QNc, QWc, Ac, Gc = 512, 1024, 1280, 1792, 2304, 2816
    out = {"x": i["x"], "ctx": i["ctx"], "final_g": i["final_g"], "sink": i["swa_sink"]}
    out["cc"] = c(np.stack([i["c"][0], i["c_ctx"]]).reshape(2, KB, P).transpose(2, 1, 0))
    out["ada"] = c(i["ada_w"].reshape(DEPTH, KB, P, MCH, 512).transpose(0, 3, 2, 1, 4).reshape(DEPTH * MCH, P, KB, 512))
    one = np.ones((D,), np.float32)
    rows = []
    for l in range(DEPTH):
        add = np.concatenate([0 * one, one, 0 * one] * 2)
        gain = np.concatenate([one, i["norm1_g"][l], one, one, i["norm2_g"][l], one])
        r = np.stack([i["ada_b"][l], add, gain]).reshape(3, MCH, 512).transpose(1, 0, 2).reshape(MCH, 1, 1536)
        rows.append(np.repeat(r, 2, 1))
    out["mrow"] = c(np.concatenate(rows))
    out["w_tok"] = c(np.stack([np.concatenate(
        [blocks(w[:, a:a + n]).reshape(P, -1) for a, n in ((VNc, 512), (KWc, 256), (QWc, 512))], 1) for w in w_in]))
    out["wqk"] = c(np.stack([np.stack([blocks(w[:, QNc + p * P:QNc + (p + 1) * P]), blocks(w[:, p * P:(p + 1) * P])], 1)
                             for w in w_in for p in range(PAIRS)]))
    out["wa"] = c(np.stack([[blocks(w[:, Ac + g * P:Ac + (g + 1) * P]) for g in range(PAIRS)] for w in w_in]))
    out["pool_w"] = c(i["pool_w"].transpose(0, 2, 1, 3))
    out["pool_scale"] = c(i["pool_scale"].reshape(DEPTH, PAIRS, P).transpose(0, 2, 1))
    wide = np.zeros((DEPTH, 8, 15, 64), np.float32)
    wide[..., 16:47] = i["na_rpb"]
    r, q = np.arange(P)[:, None, None] // QC, np.arange(P)[:, None, None] % QC
    kr, w = np.arange(ROWS)[None, :, None], np.arange(TW)[None, None, :]
    out["rpb"] = c(wide[:, :, kr - r + ROWS - 1, w - q + 15].transpose(0, 2, 1, 3, 4))
    gb = []
    for l in range(DEPTH):
        for j in range(KB):
            cols = slice(j * P, (j + 1) * P)
            gates = [blocks(w_in[l][:, Gc + b * D + j * P:Gc + b * D + (j + 1) * P]) for b in range(3)]
            outs = [i[f"w_branch_{b}"][l][:, cols].reshape(PAIRS, P, P).transpose(1, 0, 2) for b in "abc"]
            gb.append(np.concatenate(gates + outs, 1))
    out["wgb"] = c(np.stack(gb))
    out["w_out"] = c(np.stack([np.stack([blocks(w[:, h * 512:(h + 1) * 512]) for h in range(2)]) for w in i["w_out"]]))
    out["wqs"] = c(np.stack([np.concatenate(
        [blocks(i["peer_wq"][l][:, b * P:(b + 1) * P]), i["peer_keys"][l, b // 2, b % 2].T[:, None, :]], 1)
        for l in range(DEPTH) for b in range(2 * HEADS)]))
    for l in range(DEPTH):
        out[f"peer_u{l}"] = c(i["peer_u"][l])
        out[f"peer_v{l}"] = c(i["peer_v"][l])
    return out


def kernel(**inputs):
    import numpy as np
    import concourse.bacc as bacc
    from concourse.bass_utils import run_bass_kernel_spmd as run

    arrays = layouts(np, {k: np.asarray(v) for k, v in inputs.items()}) | constants(np)
    nc = bacc.Bacc("TRN2", target_bir_lowering=False, num_devices=1)
    t = {k: nc.dram_tensor("in_" + k, a.shape, mybir.dt.from_np(a.dtype), kind="ExternalInput").ap() for k, a in arrays.items()}
    t["mods_d"] = nc.dram_tensor("mods_d", (DEPTH * MCH, 2, 512), F32).ap()
    t["vn_d"] = nc.dram_tensor("vn_d", (DEPTH, TOK, 512), F32).ap()
    t["out"] = nc.dram_tensor("out_0", (1, SEQ, D), F32, kind="ExternalOutput").ap()
    for name in ("peer_u", "peer_v"):
        t[name] = [t[f"{name}{l}"] for l in range(DEPTH)]
    build(nc, t)
    r = run(nc, [{"in_" + k: a for k, a in arrays.items()}], core_ids=[0])
    return r.results[0]["out_0"]
```
